# Optimizing a Trainium2 kernel written in Bass

```python
import jax
import jax.numpy as jnp
from jax import lax
import numpy as np

D_MODEL = 1024
BATCH = 1
SEQ = 2048
DEPTH = 1

HEAD_DIM = 64
H_TOTAL = D_MODEL // HEAD_DIM
H_RET = H_TOTAL // 4
H_HGRN = (H_TOTAL - H_RET) // 2
H_FOX = H_TOTAL - H_RET - H_HGRN
D_HGRN = H_HGRN * HEAD_DIM
D_FOX = H_FOX * HEAD_DIM
D_RET = H_RET * HEAD_DIM
D_MIX = D_HGRN + D_FOX + D_RET
IN_COLS = 4 * D_HGRN + 4 * D_FOX + H_FOX + 4 * D_RET
D_FF = 2816
CONV_W = 3
CHUNK = 64
Q_BLOCK = 128
ROPE_BASE = 10000.0
EPS = 1e-6
MIN_FORGET = 1e-12
MASK_VALUE = -1e30

kernel_name = "hymba_style_hgrn2_fox_retnet_convffn"

def rmsnorm(x, gain):
    xf = x.astype(jnp.float32)
    y = xf * lax.rsqrt(jnp.mean(xf * xf, axis=-1, keepdims=True) + EPS)
    return (y * gain.astype(jnp.float32)).astype(x.dtype)

def heads(a, n_heads):
    return a.astype(jnp.float32).reshape(a.shape[0], a.shape[1], n_heads, HEAD_DIM)

def to_chunks(a):
    b, t, h, d = a.shape
    return a.reshape(b, t // CHUNK, CHUNK, h, d).transpose(1, 0, 3, 2, 4)

def from_chunks(a):
    n, b, h, c, d = a.shape
    return a.transpose(1, 0, 3, 2, 4).reshape(b, n * c, h, d)

def rotary_tables(t):
    inv_freq = 1.0 / (ROPE_BASE ** (jnp.arange(0, HEAD_DIM, 2, dtype=jnp.float32) / HEAD_DIM))
    ang = jnp.arange(t, dtype=jnp.float32)[:, None] * inv_freq[None, :]
    return jnp.cos(ang), jnp.sin(ang)

def apply_rotary(x, cos, sin):
    x1, x2 = jnp.split(x, 2, axis=-1)
    c = cos[None, :, None, :]
    s = sin[None, :, None, :]
    return jnp.concatenate([x1 * c - x2 * s, x1 * s + x2 * c], axis=-1)

def hgrn2_mixer(q_in, f_in, i_in, g_in, lb, out_gain):
    b = q_in.shape[0]
    q = heads(q_in, H_HGRN)
    v = heads(i_in, H_HGRN)
    z = heads(f_in, H_HGRN)
    lb = lb.astype(jnp.float32).reshape(H_HGRN, HEAD_DIM)
    f = lb + (1.0 - lb) * jax.nn.sigmoid(z)
    log_f = jnp.log(jnp.maximum(f, MIN_FORGET))
    k = (1.0 - lb) * jax.nn.sigmoid(-z)
    causal = jnp.tril(jnp.ones((CHUNK, CHUNK), dtype=bool))[:, :, None]

    def step(S, inp):
        qc, kc, vc, lfc = inp
        cum = jnp.cumsum(lfc, axis=2)
        diff = cum[:, :, :, None, :] - cum[:, :, None, :, :]
        decay = jnp.where(causal, jnp.exp(jnp.where(causal, diff, 0.0)), 0.0)
        scores = jnp.einsum('bhtk,bhtsk,bhsk->bhts', qc, decay, kc)
        o = (jnp.einsum('bhts,bhsv->bhtv', scores, vc)
             + jnp.einsum('bhtk,bhkv->bhtv', qc * jnp.exp(cum), S))
        last = cum[:, :, -1:, :]
        S = (jnp.exp(last[:, :, 0, :, None]) * S
             + jnp.einsum('bhsk,bhsv->bhkv', kc * jnp.exp(last - cum), vc))
        return S, o

    S0 = jnp.zeros((b, H_HGRN, HEAD_DIM, HEAD_DIM), jnp.float32)
    _, o = lax.scan(step, S0, (to_chunks(q), to_chunks(k), to_chunks(v), to_chunks(log_f)))
    o = from_chunks(o)
    o = rmsnorm(o, out_gain) * jax.nn.silu(heads(g_in, H_HGRN))
    return o.reshape(b, -1, D_HGRN)

def fox_mixer(q_in, k_in, v_in, f_in, g_in, b_f, q_gain, k_gain):
    b, t, _ = q_in.shape
    q = rmsnorm(heads(q_in, H_FOX), q_gain).transpose(0, 2, 1, 3)
    k = rmsnorm(heads(k_in, H_FOX), k_gain).transpose(0, 2, 1, 3)
    v = heads(v_in, H_FOX).transpose(0, 2, 1, 3)
    log_f = jax.nn.log_sigmoid(f_in.astype(jnp.float32) + b_f.astype(jnp.float32))
    F = jnp.cumsum(log_f, axis=1).transpose(0, 2, 1)
    scale = HEAD_DIM ** -0.5
    outs = []
    for blk in range(t // Q_BLOCK):
        t0, t1 = blk * Q_BLOCK, (blk + 1) * Q_BLOCK
        logits = (jnp.einsum('bhtd,bhsd->bhts', q[:, :, t0:t1], k[:, :, :t1]) * scale
                  + (F[:, :, t0:t1, None] - F[:, :, None, :t1]))
        mask = (t0 + jnp.arange(Q_BLOCK))[:, None] >= jnp.arange(t1)[None, :]
        p = jax.nn.softmax(jnp.where(mask, logits, MASK_VALUE), axis=-1)
        outs.append(jnp.einsum('bhts,bhsd->bhtd', p, v[:, :, :t1]))
    o = jnp.concatenate(outs, axis=2).transpose(0, 2, 1, 3)
    o = o * jax.nn.sigmoid(heads(g_in, H_FOX))
    return o.reshape(b, t, D_FOX)

def retention_mixer(q_in, k_in, v_in, g_in, out_gain, cos, sin):
    b = q_in.shape[0]
    q = apply_rotary(heads(q_in, H_RET), cos, sin)
    k = apply_rotary(heads(k_in, H_RET), cos, sin) * (HEAD_DIM ** -0.5)
    v = heads(v_in, H_RET)
    log_gamma = jnp.log1p(-jnp.exp2(-5.0 - jnp.arange(H_RET, dtype=jnp.float32)))
    pos = jnp.arange(CHUNK, dtype=jnp.float32)
    rel = pos[:, None] - pos[None, :]
    intra = jnp.where(rel >= 0, jnp.exp(log_gamma[:, None, None] * jnp.maximum(rel, 0.0)), 0.0)
    q_scale = jnp.exp(log_gamma[:, None] * (pos + 1.0))[:, :, None]
    k_scale = jnp.exp(log_gamma[:, None] * (CHUNK - 1.0 - pos))[:, :, None]
    chunk_decay = jnp.exp(log_gamma * CHUNK)[:, None, None]

    def step(R, inp):
        qc, kc, vc = inp
        scores = jnp.einsum('bhtd,bhsd->bhts', qc, kc) * intra
        o = (jnp.einsum('bhts,bhsv->bhtv', scores, vc)
             + jnp.einsum('bhtd,bhdv->bhtv', qc * q_scale, R))
        R = chunk_decay * R + jnp.einsum('bhsd,bhsv->bhdv', kc * k_scale, vc)
        return R, o

    R0 = jnp.zeros((b, H_RET, HEAD_DIM, HEAD_DIM), jnp.float32)
    _, o = lax.scan(step, R0, (to_chunks(q), to_chunks(k), to_chunks(v)))
    o = from_chunks(o)
    o = rmsnorm(o, out_gain) * jax.nn.silu(heads(g_in, H_RET))
    return o.reshape(b, -1, D_RET)

def conv_gated_mlp(h, w_up, conv_w, conv_b, w_down):
    t = h.shape[1]
    u = h @ w_up
    u_pad = jnp.pad(u, ((0, 0), (CONV_W - 1, 0), (0, 0)))
    acc = conv_b
    for j in range(CONV_W):
        acc = acc + conv_w[j] * u_pad[:, j:j + t]
    gate, val = jnp.split(acc, 2, axis=-1)
    return (jax.nn.silu(gate) * val) @ w_down

def setup_inputs(seed: int = 0) -> dict:
    key = jax.random.key(seed)
    ks = jax.random.split(key, 20)
    f32 = jnp.float32

    def gain(k, shape):
        return 1.0 + 0.02 * jax.random.normal(k, shape, f32)

    x = jax.random.normal(ks[0], (BATCH, SEQ, D_MODEL), f32)
    w_in = jax.random.normal(ks[1], (DEPTH, D_MODEL, IN_COLS), f32) * D_MODEL ** -0.5
    b_fox_f = jax.random.uniform(ks[2], (DEPTH, H_FOX), f32, 1.0, 4.0)
    fox_q_gain = gain(ks[3], (DEPTH, HEAD_DIM))
    fox_k_gain = gain(ks[4], (DEPTH, HEAD_DIM))
    hgrn_lb = 1.0 + 0.1 * jax.random.normal(ks[5], (DEPTH, D_HGRN), f32)
    hgrn_out_gain = gain(ks[6], (DEPTH, H_HGRN, HEAD_DIM))
    ret_out_gain = gain(ks[7], (DEPTH, H_RET, HEAD_DIM))
    w_out = jax.random.normal(ks[8], (DEPTH, D_MIX, D_MODEL), f32) * D_MIX ** -0.5
    g_mix_pre = gain(ks[9], (DEPTH, D_MODEL))
    g_mix_post = gain(ks[10], (DEPTH, D_MODEL))
    w_up = jax.random.normal(ks[11], (DEPTH, D_MODEL, 2 * D_FF), f32) * D_MODEL ** -0.5
    conv_w = 0.2 * jax.random.normal(ks[12], (DEPTH, CONV_W, 2 * D_FF), f32)
    conv_w = conv_w.at[:, CONV_W - 1, :].add(1.0)
    conv_b = 0.02 * jax.random.normal(ks[13], (DEPTH, 2 * D_FF), f32)
    w_down = jax.random.normal(ks[14], (DEPTH, D_FF, D_MODEL), f32) * D_FF ** -0.5
    g_ffn_pre = gain(ks[15], (DEPTH, D_MODEL))
    g_ffn_post = gain(ks[16], (DEPTH, D_MODEL))
    return {"x": x, "w_in": w_in, "b_fox_f": b_fox_f, "fox_q_gain": fox_q_gain,
            "fox_k_gain": fox_k_gain, "hgrn_lb": hgrn_lb, "hgrn_out_gain": hgrn_out_gain,
            "ret_out_gain": ret_out_gain, "w_out": w_out, "g_mix_pre": g_mix_pre,
            "g_mix_post": g_mix_post, "w_up": w_up, "conv_w": conv_w, "conv_b": conv_b,
            "w_down": w_down, "g_ffn_pre": g_ffn_pre, "g_ffn_post": g_ffn_post}

def reference(x, w_in, b_fox_f, fox_q_gain, fox_k_gain, hgrn_lb, hgrn_out_gain, ret_out_gain,
              w_out, g_mix_pre, g_mix_post, w_up, conv_w, conv_b, w_down, g_ffn_pre, g_ffn_post):
    t = x.shape[1]
    widths = [D_HGRN] * 4 + [D_FOX] * 3 + [H_FOX] + [D_FOX] + [D_RET] * 4
    splits = []
    off = 0
    for w in widths[:-1]:
        off += w
        splits.append(off)
    p_lb = jax.nn.softmax(hgrn_lb.astype(jnp.float32), axis=0)
    lower_bounds = jnp.cumsum(p_lb, axis=0) - p_lb[0]
    cos, sin = rotary_tables(t)
    for l in range(DEPTH):
        h = rmsnorm(x, g_mix_pre[l])
        (a_q, a_f, a_i, a_g,
         b_q, b_k, b_v, b_f, b_g,
         c_q, c_k, c_v, c_g) = jnp.split(h @ w_in[l], splits, axis=-1)
        o_a = hgrn2_mixer(a_q, a_f, a_i, a_g, lower_bounds[l], hgrn_out_gain[l])
        o_b = fox_mixer(b_q, b_k, b_v, b_f, b_g, b_fox_f[l], fox_q_gain[l], fox_k_gain[l])
        o_c = retention_mixer(c_q, c_k, c_v, c_g, ret_out_gain[l], cos, sin)
        mixed = jnp.concatenate([o_a, o_b, o_c], axis=-1).astype(x.dtype) @ w_out[l]
        x = x + rmsnorm(mixed, g_mix_post[l])
        h = rmsnorm(x, g_ffn_pre[l])
        x = x + rmsnorm(conv_gated_mlp(h, w_up[l], conv_w[l], conv_b[l], w_down[l]), g_ffn_post[l])
    return x


_drawn_inputs = setup_inputs


def setup_inputs(seed=0):
    import zlib

    import numpy as np

    out = dict(_drawn_inputs(seed))
    spreads = {}
    factors = {'fox_q_gain': 8.0,
     'fox_k_gain': 8.0,
     'hgrn_out_gain': 4.222,
     'ret_out_gain': 5.522,
     'g_mix_post': 3.542,
     'conv_b': 3.645,
     'g_ffn_pre': 3.437,
     'g_ffn_post': 4.948}
    for name, (base, spread) in spreads.items():
        noise = np.random.default_rng([zlib.crc32(name.encode()), seed]).standard_normal(out[name].shape)
        drawn = base * np.exp(spread * noise) if base else spread * noise
        out[name] = jnp.asarray(drawn.astype(out[name].dtype))
    for name, factor in factors.items():
        out[name] = (out[name] * factor).astype(out[name].dtype)
    return out
```

```python
from contextlib import ExitStack

import numpy as np

import concourse.bass as bass
from concourse import mybir

F32 = mybir.dt.float32
F32R = mybir.dt.float32r
BF16 = mybir.dt.bfloat16
I32 = mybir.dt.int32
ACT = mybir.ActivationFunctionType
ALU = mybir.AluOpType
AX = mybir.AxisListType

P = 128
D = 1024
T = 2048
HD = 64
NT = T // P
KB = D // P
NQ = T // 512
DFF = 2816
FB = DFF // P
EPS = 1e-6
MIN_FORGET = 1e-12
NEG = -1e30
AQ, AF, AG, BQ, BK, CQ, CK, CG, BG, BF, NPB = 0, 3, 6, 9, 12, 15, 17, 19, 21, 24, 25
NFIRST = 9
NA, NC = 3, 2
LEVELS = [64, 32, 16, 8, 4, 2, 1]


def f32(ap):
    return ap.bitcast(F32)


def done(n):
    return n + 3


def free(n):
    return n + 1


def later(n, first):
    return not isinstance(n, int) or n >= first


def before_last(c):
    return not (isinstance(c, int) and c == NT - 1)


def over_pairs(eng, total, a, b):
    a(0, 0, 0)
    with eng.Fori(0, total // 2 - 1) as i:
        a(i * 2 + 1, 1, i)
        b(i * 2, 0, i)
        a(i * 2 + 2, 0, i + 1)
        b(i * 2 + 1, 1, i)
    a(total - 1, 1, total // 2 - 1)
    b(total - 2, 0, total // 2 - 1)
    b(total - 1, 1, total // 2 - 1)


def over_three(eng, total, a, b, c):
    a(0, 0, 0)
    a(1, 1, 0)
    b(0, 0, 0)
    with eng.Fori(0, total // 2 - 1) as i:
        a(i * 2 + 2, 0, i + 1)
        b(i * 2 + 1, 1, i)
        c(i * 2, 0, i)
        a(i * 2 + 3, 1, i + 1)
        b(i * 2 + 2, 0, i + 1)
        c(i * 2 + 1, 1, i)
    b(total - 1, 1, total // 2 - 1)
    c(total - 2, 0, total // 2 - 1)
    c(total - 1, 1, total // 2 - 1)


def loaded(i):
    return i * 16 + 16


LN_EXP_TABLES = 6


def load_ln_exp_tables(nc, act):
    act.add_instruction(mybir.InstLoadActFuncSet(name=nc.get_next_instruction_name(), engine=mybir.EngineType.Activation,
                                                 act_func_set_id=LN_EXP_TABLES, ins=[], outs=[]))


def maker(nc, ctx, tag):
    sems = []

    def sem(n):
        sems.append(nc.alloc_semaphore(f"{tag}_{n}"))
        return sems[-1]

    def retire():
        nc.clear_and_free_semaphores(sems)
        nc.all_engine_barrier()

    ctx.callback(retire)
    return (lambda n, s, d=F32: ctx.enter_context(nc.sbuf_tensor(f"{tag}_{n}", s, d)),
            lambda n, s, d=F32: ctx.enter_context(nc.psum_tensor(f"{tag}_{n}", s, d)), sem)


def normalise_transpose(nc, g, tag, src, gain, hT_hi, hT_lo, tiles):
    with ExitStack() as ctx:
        sb, ps, sem = maker(nc, ctx, tag)
        x_in, xn = sb("x_in", [P, 2, D]), sb("xn", [P, 2, D])
        junk = sb("junk", [P, D])
        gain_b, ident, eps = sb("gain_b", [P, D]), sb("ident", [P, P]), sb("eps", [P, 1])
        rs = sb("rs", [P, 2, 4])
        tp = [ps(f"tp{b}", [P, KB, P]) for b in range(2)]
        consts, eps_ok = sem("consts"), sem("eps_ok")
        x_ld = [sem(f"x_ld{b}") for b in range(2)]
        act_step, rstd, xn_ok, tp_ok, hi_ok, lo_ok = (
            sem(n) for n in ("act_step", "rstd", "xn_ok", "tp_ok", "hi_ok", "lo_ok"))
        blk = ctx.enter_context(nc.Block())

        def cols(i, b):
            return bass.ds(i * 256 + b * P, P)

        @blk.sync
        def _(sp):
            sp.dma_start(gain_b[:], gain[0:1, :].broadcast_to([P, D])).then_inc(consts, 16)
            sp.dma_start(ident[:], g["c_ident"]).then_inc(consts, 16)
            with sp.Fori(0, tiles // 2) as i:
                for b in range(2):
                    sp.wait_ge(xn_ok, free(i * 2 + b))
                    sp.dma_start(x_in[:, b, :], src[cols(i, b), :]).then_inc(x_ld[b], 16)

        @blk.scalar
        def _(act):
            load_ln_exp_tables(nc, act)
            act.wait_ge(eps_ok, 1)

            def stats(i, b):
                act.wait_ge(x_ld[b], loaded(i))
                act.wait_ge(xn_ok, free(i * 2 + b))
                act.activation(junk[:], x_in[:, b, :], ACT.Square,
                               accum_out=rs[:, b, 0:1]).then_inc(act_step, 1)
                act.wait_ge(act_step, i * 4 + 2 * b + 1)
                act.activation(rs[:, b, 1:2], rs[:, b, 0:1], ACT.Ln, scale=1.0 / D,
                               bias=eps[:, 0:1]).then_inc(act_step, 1)
                act.wait_ge(act_step, i * 4 + 2 * b + 2)
                act.activation(rs[:, b, 2:3], rs[:, b, 1:2], ACT.Exp, scale=-0.5).then_inc(rstd, 1)

            def hi(i, b):
                act.wait_ge(tp_ok, done(i * 2 + b))
                act.activation(hT_hi[:, :, cols(i, b)], tp[b][:], ACT.Copy).then_inc(hi_ok, 1)

            stats(0, 0)
            with act.Fori(0, tiles // 2 - 1) as i:
                stats(i, 1)
                hi(i, 0)
                stats(i + 1, 0)
                hi(i, 1)
            stats(tiles // 2 - 1, 1)
            hi(tiles // 2 - 1, 0)
            hi(tiles // 2 - 1, 1)

        @blk.vector
        def _(dve):
            dve.sem_inc(xn_ok, 2)
            dve.sem_inc(tp_ok, 2)
            dve.sem_inc(lo_ok, 2)
            dve.memset(eps[:], EPS).then_inc(eps_ok, 1)
            dve.wait_ge(consts, 32)

            def scale(i, b):
                dve.wait_ge(rstd, i * 2 + b + 1)
                dve.wait_ge(tp_ok, free(i * 2 + b))
                dve.scalar_tensor_tensor(out=xn[:, b, :], in0=x_in[:, b, :], scalar=rs[:, b, 2:3],
                                         in1=gain_b[:], op0=ALU.mult, op1=ALU.mult).then_inc(xn_ok, 1)

            def lo(i, b):
                dve.wait_ge(hi_ok, i * 2 + b + 1)
                dve.tensor_tensor(hT_lo[:, :, cols(i, b)], tp[b][:], f32(hT_hi[:, :, cols(i, b)]),
                                  ALU.subtract).then_inc(lo_ok, 1)

            scale(0, 0)
            with dve.Fori(0, tiles // 2 - 1) as i:
                scale(i, 1)
                lo(i, 0)
                scale(i + 1, 0)
                lo(i, 1)
            scale(tiles // 2 - 1, 1)
            lo(tiles // 2 - 1, 0)
            lo(tiles // 2 - 1, 1)

        @blk.tensor
        def _(pe):
            pe.wait_ge(consts, 32)
            with pe.Fori(0, tiles // 2) as i:
                for b in range(2):
                    pe.wait_ge(xn_ok, done(i * 2 + b))
                    pe.wait_ge(lo_ok, free(i * 2 + b))
                    for k in range(KB):
                        mm = pe.transpose(tp[b][:, k, :], xn[:, b, k * P:(k + 1) * P], ident[:])
                    mm.then_inc(tp_ok, 1)


def three_passes(pe, out, l_hi, l_lo, r_hi, r_lo, first, last):
    pe.matmul(out, l_hi, r_hi, start=first, stop=False)
    pe.matmul(out, l_hi, r_lo, start=False, stop=False)
    return pe.matmul(out, l_lo, r_hi, start=False, stop=last)


def project(nc, g, hT_hi, hT_lo):
    PAIRS = NFIRST // 2
    with ExitStack() as ctx:
        sb, ps, sem = maker(nc, ctx, "pj")
        w_raw = sb("w_raw", [P, 2, KB, P])
        w_hi, w_lo = sb("w_hi", [P, 2, KB, P], F32R), sb("w_lo", [P, 2, KB, P], F32R)
        stage = sb("stage", [P, 2, T])
        acc = [ps(f"acc{b}", [P, NQ, 512]) for b in range(2)]
        w_ld = [sem(f"w_ld{b}") for b in range(2)]
        stored = [sem(f"stored{b}") for b in range(2)]
        hi_ok, lo_ok, mm_ok, ev_ok = (sem(n) for n in ("hi_ok", "lo_ok", "mm_ok", "ev_ok"))
        blk = ctx.enter_context(nc.Block())

        @blk.sync
        def _(sp):
            def load(i, b):
                sp.wait_ge(lo_ok, free(i * 2 + b))
                sp.dma_start(w_raw[:, b], g["w_blk"][i * 2 + b]).then_inc(w_ld[b], 16)

            with sp.Fori(0, PAIRS) as i:
                load(i, 0)
                load(i, 1)
            load(PAIRS, 0)

        @blk.scalar
        def _(act):
            def split_hi(i, b):
                act.wait_ge(w_ld[b], loaded(i))
                act.wait_ge(mm_ok, free(i * 2 + b))
                act.activation(w_hi[:, b], w_raw[:, b], ACT.Copy).then_inc(hi_ok, 1)

            def evacuate(i, b, func):
                act.wait_ge(mm_ok, done(i * 2 + b))
                act.wait_ge(stored[b], loaded(i))
                act.activation(stage[:, b, :], acc[b][:].rearrange("p a n -> p (a n)"), func).then_inc(ev_ok, 1)
                act.wait_ge(ev_ok, done(i * 2 + b))
                act.dma_start(g["projT"][i * 2 + b], stage[:, b, :]).then_inc(stored[b], 16)

            def pair(i, func):
                split_hi(i, 1)
                evacuate(i, 0, func)
                split_hi(i + 1, 0)
                evacuate(i, 1, func)

            split_hi(0, 0)
            with act.Fori(0, AG // 2) as i:
                pair(i, ACT.Copy)
            pair(AG // 2, ACT.Silu)
            evacuate(PAIRS, 0, ACT.Silu)
            act.wait_ge(stored[0], loaded(PAIRS + 1))
            act.wait_ge(stored[1], loaded(PAIRS))

        @blk.vector
        def _(dve):
            for ring in (lo_ok, mm_ok, ev_ok):
                dve.sem_inc(ring, 2)
            for b in range(2):
                dve.sem_inc(stored[b], 16)

            def split_lo(i, b):
                dve.wait_ge(hi_ok, i * 2 + b + 1)
                dve.tensor_tensor(w_lo[:, b], w_raw[:, b], f32(w_hi[:, b]), ALU.subtract).then_inc(lo_ok, 1)

            with dve.Fori(0, PAIRS) as i:
                split_lo(i, 0)
                split_lo(i, 1)
            split_lo(PAIRS, 0)

        @blk.tensor
        def _(pe):
            def products(i, b):
                pe.wait_ge(lo_ok, done(i * 2 + b))
                pe.wait_ge(ev_ok, free(i * 2 + b))
                for q in range(NQ):
                    cols = slice(q * 512, (q + 1) * 512)
                    for k in range(KB):
                        mm = three_passes(pe, acc[b][:, q, :], w_hi[:, b, k], w_lo[:, b, k],
                                          hT_hi[:, k, cols], hT_lo[:, k, cols], k == 0, k == KB - 1)
                mm.then_inc(mm_ok, 1)

            with pe.Fori(0, PAIRS) as i:
                products(i, 0)
                products(i, 1)
            products(PAIRS, 0)


def project_values(nc, g, hT_hi, hT_lo):
    W = 512
    with ExitStack() as ctx:
        sb, ps, sem = maker(nc, ctx, "pv")
        w_raw = sb("w_raw", [P, 2, W])
        w_hi, w_lo = sb("w_hi", [P, KB, W], F32R), sb("w_lo", [P, KB, W], F32R)
        stage = sb("stage", [P, 2, W])
        acc = [ps(f"acc{b}", [P, W]) for b in range(2)]
        w_ld = [sem(f"w_ld{b}") for b in range(2)]
        stored = [sem(f"stored{b}") for b in range(2)]
        hi_ok, lo_ok, mm_ok, ev_ok = (sem(n) for n in ("hi_ok", "lo_ok", "mm_ok", "ev_ok"))
        blk = ctx.enter_context(nc.Block())

        @blk.sync
        def _(sp):
            with sp.Fori(0, 2) as c:
                for k in range(KB):
                    sp.wait_ge(lo_ok, free(c * KB + k))
                    sp.dma_start(w_raw[:, k % 2, :], g["w_v"][c, :, k, :]).then_inc(w_ld[k % 2], 16)

        @blk.scalar
        def _(act):
            with act.Fori(0, 2) as c:
                act.wait_ge(mm_ok, c * NT + 2)
                for k in range(KB):
                    act.wait_ge(w_ld[k % 2], (c * (KB // 2) + k // 2 + 1) * 16)
                    act.activation(w_hi[:, k, :], w_raw[:, k % 2, :], ACT.Copy).then_inc(hi_ok, 1)
                for t in range(NT):
                    act.wait_ge(mm_ok, done(c * NT + t))
                    act.wait_ge(stored[t % 2], loaded(c * (NT // 2) + t // 2))
                    act.activation(stage[:, t % 2, :], acc[t % 2][:], ACT.Copy).then_inc(ev_ok, 1)
                    act.wait_ge(ev_ok, done(c * NT + t))
                    act.dma_start(g["v_tok"][t * P:(t + 1) * P, bass.ds(c * W, W)], stage[:, t % 2, :]).then_inc(stored[t % 2], 16)
            for b in range(2):
                act.wait_ge(stored[b], loaded(NT))

        @blk.vector
        def _(dve):
            for ring in (lo_ok, mm_ok, ev_ok):
                dve.sem_inc(ring, 2)
            for b in range(2):
                dve.sem_inc(stored[b], 16)
            with dve.Fori(0, 2) as c:
                for k in range(KB):
                    dve.wait_ge(hi_ok, c * KB + k + 1)
                    dve.tensor_tensor(w_lo[:, k, :], w_raw[:, k % 2, :], f32(w_hi[:, k, :]),
                                      ALU.subtract).then_inc(lo_ok, 1)

        @blk.tensor
        def _(pe):
            with pe.Fori(0, 2) as c:
                for t in range(NT):
                    rows = slice(t * P, (t + 1) * P)
                    pe.wait_ge(ev_ok, free(c * NT + t))
                    for k in range(KB):
                        if t == 0:
                            pe.wait_ge(lo_ok, done(c * KB + k))
                        mm = three_passes(pe, acc[t % 2][:], hT_hi[:, k, rows], hT_lo[:, k, rows],
                                          w_hi[:, k, :], w_lo[:, k, :], k == 0, k == KB - 1)
                    mm.then_inc(mm_ok, 1)


def fox_prepare(nc, g):
    with ExitStack() as ctx:
        sb, ps, sem = maker(nc, ctx, "fp")
        fl, fa, fm, ones6 = sb("fl", [6, T]), sb("fa", [6, T]), sb("fm", [6, T]), sb("ones6", [6, T])
        f_hi, f_lo = sb("f_hi", [6, T], F32R), sb("f_lo", [6, T], F32R)
        bf, one = sb("bf", [6, 1]), sb("one", [6, 1])
        headsum, eps, gains = sb("headsum", [P, P]), sb("eps", [P, 1]), sb("gains", [P, 2])
        x_in, sq, xn = sb("x_in", [P, 2, T]), sb("sq", [P, 2, T]), sb("xn", [P, 2, T])
        x_hi, x_lo = sb("x_hi", [P, 2, T], F32R), sb("x_lo", [P, 2, T], F32R)
        ss = [ps(f"ss{b}", [P, NQ, 512]) for b in range(2)]
        x_ld = [sem(f"x_ld{b}") for b in range(2)]
        hi_st, lo_st = [sem(f"hi_st{b}") for b in range(2)], [sem(f"lo_st{b}") for b in range(2)]
        consts, setup, fa_step, fm_step, f_out = (sem(n) for n in ("consts", "setup", "fa_step", "fm_step", "f_out"))
        sq_ok, ss_ok, ln_ok, r_ok, xn_ok, hi_ok, lo_ok = (
            sem(n) for n in ("sq_ok", "ss_ok", "ln_ok", "r_ok", "xn_ok", "hi_ok", "lo_ok"))
        blk = ctx.enter_context(nc.Block())

        @blk.sync
        def _(sp):
            sp.dma_start(fl[:], g["projT"][BF, 0:6, :]).then_inc(consts, 16)
            sp.dma_start(bf[:], g["b_f"]).then_inc(consts, 16)
            sp.dma_start(headsum[:], g["c_headsum"]).then_inc(consts, 16)
            sp.dma_start(gains[:], g["fox_gain"]).then_inc(consts, 16)
            with sp.Fori(0, 3) as i:
                for b in range(2):
                    sp.wait_ge(xn_ok, free(i * 2 + b))
                    sp.dma_start(x_in[:, b, :], g["projT"][i + (BQ + 3 * b)]).then_inc(x_ld[b], 16)
                for b in range(2):
                    sp.wait_ge(lo_ok, i * 2 + b + 1)
                    sp.dma_start(g["qk_lo"][i + 3 * b], f32(x_lo[:, b, :])).then_inc(lo_st[b], 16)
            sp.wait_ge(fm_step, 5)
            sp.dma_start(g["negF"][:, 0, :], f32(f_hi[:])).then_inc(f_out, 16)
            sp.dma_start(g["negF"][:, 1, :], f32(f_lo[:])).then_inc(f_out, 16)
            sp.wait_ge(f_out, 32)
            for b in range(2):
                sp.wait_ge(lo_st[b], loaded(3))

        @blk.scalar
        def _(act):
            load_ln_exp_tables(nc, act)
            act.wait_ge(consts, 64)
            act.wait_ge(setup, 3)
            act.activation(fa[:], fl[:], ACT.Abs, bias=bf[:, 0:1]).then_inc(fa_step, 1)
            act.wait_ge(fa_step, 1)
            act.activation(fa[:], fa[:], ACT.Exp, scale=-1.0).then_inc(fa_step, 1)
            act.wait_ge(fa_step, 2)
            act.activation(fa[:], fa[:], ACT.Ln, bias=one[:, 0:1]).then_inc(fa_step, 1)

            def square(i, b):
                act.wait_ge(x_ld[b], loaded(i))
                act.wait_ge(xn_ok, free(i * 2 + b))
                act.activation(sq[:, b, :], x_in[:, b, :], ACT.Square).then_inc(sq_ok, 1)

            def rest(i, b):
                act.wait_ge(ss_ok, i * 2 + b + 1)
                act.activation(sq[:, b, :], ss[b][:].rearrange("p a n -> p (a n)"), ACT.Ln, scale=1.0 / HD,
                               bias=eps[:, 0:1]).then_inc(ln_ok, 1)
                act.wait_ge(ln_ok, i * 2 + b + 1)
                act.activation(sq[:, b, :], sq[:, b, :], ACT.Exp, scale=-0.5).then_inc(r_ok, 1)
                act.wait_ge(hi_st[b], loaded(i))
                act.wait_ge(xn_ok, done(i * 2 + b))
                act.activation(x_hi[:, b, :], xn[:, b, :], ACT.Copy).then_inc(hi_ok, 1)
                act.wait_ge(hi_ok, i * 2 + b + 1)
                act.dma_start(g["qk_hi"][i + 3 * b], f32(x_hi[:, b, :])).then_inc(hi_st[b], 16)

            with act.Fori(0, 3) as i:
                square(i, 0)
                square(i, 1)
                rest(i, 0)
                rest(i, 1)
            for b in range(2):
                act.wait_ge(hi_st[b], loaded(3))

        @blk.vector
        def _(dve):
            dve.sem_inc(xn_ok, 2)
            for b in range(2):
                dve.sem_inc(hi_st[b], 16)
                dve.sem_inc(lo_st[b], 16)
            dve.memset(one[:], 1.0).then_inc(setup, 1)
            dve.memset(ones6[:], 1.0).then_inc(setup, 1)
            dve.memset(eps[:], EPS).then_inc(setup, 1)
            dve.wait_ge(consts, 64)
            dve.tensor_scalar(fm[:], fl[:], bf[:, 0:1], 0.0, ALU.add, ALU.min).then_inc(fm_step, 1)
            dve.wait_ge(fm_step, 1)
            dve.wait_ge(fa_step, 3)
            dve.tensor_tensor(fm[:], fa[:], fm[:], ALU.subtract).then_inc(fm_step, 1)
            dve.wait_ge(fm_step, 2)
            dve.tensor_tensor_scan(fa[:], ones6[:], fm[:], 0.0, ALU.mult, ALU.add).then_inc(fm_step, 1)
            dve.wait_ge(fm_step, 3)
            dve.tensor_copy(f_hi[:], fa[:]).then_inc(fm_step, 1)
            dve.wait_ge(fm_step, 4)
            dve.tensor_tensor(f_lo[:], fa[:], f32(f_hi[:]), ALU.subtract).then_inc(fm_step, 1)
            dve.tensor_scalar(gains[:, 0:1], gains[:, 0:1], HD ** -0.5, None, ALU.mult).then_inc(setup, 1)
            dve.wait_ge(setup, 4)
            with dve.Fori(0, 3) as i:
                for b in range(2):
                    dve.wait_ge(r_ok, i * 2 + b + 1)
                    dve.scalar_tensor_tensor(out=xn[:, b, :], in0=x_in[:, b, :], scalar=gains[:, b:b + 1],
                                             in1=sq[:, b, :], op0=ALU.mult, op1=ALU.mult).then_inc(xn_ok, 1)
                    dve.wait_ge(hi_ok, i * 2 + b + 1)
                    dve.wait_ge(lo_st[b], loaded(i))
                    dve.tensor_tensor(x_lo[:, b, :], xn[:, b, :], f32(x_hi[:, b, :]), ALU.subtract).then_inc(lo_ok, 1)

        @blk.tensor
        def _(pe):
            pe.wait_ge(consts, 64)
            with pe.Fori(0, 3) as i:
                for b in range(2):
                    pe.wait_ge(sq_ok, i * 2 + b + 1)
                    for q in range(NQ):
                        mm = pe.matmul(ss[b][:, q, :], headsum[:], sq[:, b, q * 512:(q + 1) * 512],
                                       start=True, stop=True)
                    mm.then_inc(ss_ok, 1)


def fox_items():
    items = []
    for q in range(NQ):
        items += [(q, [2 * m, 2 * m + 1], 0) for m in range(2 * q)]
        items += [(q, [4 * q + m], P * m) for m in range(4)]
    return items


def fox_chunks():
    return [(t, c, c * 512, min((t + 1) * P, (c + 1) * 512)) for t in range(NT) for c in range(t // 4 + 1)]


def fox_attention(nc, g):
    items, chunks = fox_items(), fox_chunks()
    NI, NCH = len(items), len(chunks)
    FIRST_CHUNK, PER_ITEM = 5, 2
    with ExitStack() as ctx:
        sb, ps, sem = maker(nc, ctx, "fx")
        both = range(2)
        K1 = [sb(f"K1{e}", [P, T], F32R) for e in both]
        Q1 = [sb(f"Q1{e}", [P, T], F32R) for e in both]
        X = [sb(f"X{e}", [68, T], F32R) for e in both]
        Y = [sb(f"Y{e}", [68, T], F32R) for e in both]
        Z = [sb(f"Z{e}", [68, T], F32R) for e in both]
        V = [sb(f"V{e}", [P, NT, P]) for e in both]
        gate, o = sb("gate", [P, T]), sb("o", [P, T])
        p = sb("p", [P, 2, 2, 512])
        rden = sb("rden", [P, 2, 512])
        mx, m1 = sb("mx", [P, NT, 4]), sb("m1", [P, NT])
        m_hl = sb("m_hl", [P, 2, NT], F32R)
        m_row = sb("m_row", [2 * NT, P])
        ident, mask, maskT = sb("ident", [P, P]), sb("mask", [P, P]), sb("maskT", [P, P])
        ident_b, mask_b, maskT_b = (sb(n, [P, P], BF16) for n in ("ident_b", "mask_b", "maskT_b"))
        sS = [ps(f"sS{b}", [P, 2, 512]) for b in both]
        s1 = [ps(f"s1{b}", [P, 512]) for b in both]
        acc = [ps(f"acc{b}", [P, 512]) for b in both]
        consts, setup, gate_ld, gate_ok, o_st = (sem(n) for n in ("consts", "setup", "gate_ld", "gate_ok", "o_st"))
        xy_ld, kq_ld = [sem(f"xy_ld{e}") for e in both], [sem(f"kq_ld{e}") for e in both]
        m_st, m_ld = sem("m_st"), [sem(f"m_ld{e}") for e in both]
        s_ok, p_ok, pv_ok, c_ok, r_ok = (sem(n) for n in ("s_ok", "p_ok", "pv_ok", "c_ok", "r_ok"))
        m_step, mt_ok, mrow_ok = sem("m_step"), sem("mt_ok"), sem("mrow_ok")
        ln_ok, rd_ok, fin_ok, o_ok = (sem(n) for n in ("ln_ok", "rd_ok", "fin_ok", "o_ok"))
        blk = ctx.enter_context(nc.Block())

        def head_loads(sp, i, e):
            rows = slice(HD * e, HD * e + HD)
            q_hi, k_hi = g["qk_hi"][i, rows, :], g["qk_hi"][i + 3, rows, :]
            q_lo, k_lo = g["qk_lo"][i, rows, :], g["qk_lo"][i + 3, rows, :]
            sp.dma_start(f32(X[e][0:HD, :]), q_hi).then_inc(xy_ld[e], 16)
            sp.dma_start(f32(Y[e][0:HD, :]), k_hi).then_inc(xy_ld[e], 16)
            sp.dma_start(f32(Y[e][HD:HD + 2, :]), g["negF"][i * 2 + e]).then_inc(xy_ld[e], 16)
            sp.dma_start(f32(K1[e][0:HD, :]), k_hi).then_inc(kq_ld[e], 16)
            sp.dma_start(f32(K1[e][HD:P, :]), k_lo).then_inc(kq_ld[e], 16)
            sp.dma_start(f32(Q1[e][0:HD, :]), q_hi).then_inc(kq_ld[e], 16)
            sp.dma_start(f32(Q1[e][HD:P, :]), q_hi).then_inc(kq_ld[e], 16)
            sp.dma_start(f32(Z[e][0:HD, :]), q_lo).then_inc(kq_ld[e], 16)
            sp.dma_start(V[e][:, :, HD * e:HD * e + HD],
                         g["v_tok"][:, bass.ds((i * 2 + e) * HD, HD)].rearrange("(n p) d -> p n d", p=P)
                         ).then_inc(kq_ld[e], 16)

        def m_rows(sp, h, i, e):
            sp.wait_ge(mrow_ok, h + 1)
            sp.dma_start(g["M_rows"][i * 2 + e].rearrange("r (n t) -> (r n) t", n=NT), m_row[:]).then_inc(m_st, 16)
            sp.wait_ge(m_st, h * 16 + 16)
            sp.dma_start(f32(Z[e][HD + 2:HD + 4, :]), g["M_rows"][i * 2 + e]).then_inc(m_ld[e], 16)

        @blk.sync
        def _(sp):
            for t, n in ((ident, "c_ident"), (mask, "c_negmask"), (maskT, "c_negmaskT")):
                sp.dma_start(t[:], g[n]).then_inc(consts, 16)
            sp.wait_ge(setup, 12)
            head_loads(sp, 0, 0)
            head_loads(sp, 0, 1)
            m_rows(sp, 0, 0, 0)

            def pair(i, last):
                sp.wait_ge(o_ok, i * 8 + 1)
                sp.dma_start(gate[:], g["projT"][i + BG]).then_inc(gate_ld, 16)
                m_rows(sp, i * 2 + 1, i, 1)
                if not last:
                    sp.wait_ge(pv_ok, i * (2 * NI) + NI)
                    head_loads(sp, i + 1, 0)
                    m_rows(sp, i * 2 + 2, i + 1, 0)
                sp.wait_ge(o_ok, i * 8 + 9)
                sp.dma_start(g["mixT"][i + 3], o[:]).then_inc(o_st, 16)
                if not last:
                    sp.wait_ge(pv_ok, i * (2 * NI) + 2 * NI)
                    head_loads(sp, i + 1, 1)

            with sp.Fori(0, 2) as i:
                pair(i, False)
            pair(2, True)
            sp.wait_ge(o_st, 16 * 4)

        @blk.scalar
        def _(act):
            load_ln_exp_tables(nc, act)

            def finish_group(n4, e, q, last_item):
                rows, dens = (slice(0, HD), slice(HD, P)) if e == 0 else (slice(HD, P), slice(0, HD))
                b = q % 2
                act.wait_ge(pv_ok, last_item + 1)
                act.wait_ge(fin_ok, n4 + 1)
                act.activation(rden[rows, b, :], acc[b][dens, :], ACT.Ln).then_inc(ln_ok, 1)
                act.wait_ge(ln_ok, n4 + 1)
                act.activation(rden[rows, b, :], rden[rows, b, :], ACT.Exp, scale=-1.0).then_inc(rd_ok, 1)

            def head(i, e):
                base = i * (2 * NI) + e * NI
                for n, (q, tiles, off) in enumerate(items):
                    act.wait_ge(s_ok, base + n + 1)
                    act.activation(p[:, n % 2, 0:len(tiles), off:512], sS[n % 2][:, 0:len(tiles), off:512],
                                   ACT.Exp).then_inc(p_ok, 1)
                    if n >= 1 and items[n - 1][0] != q:
                        finish_group(i * 8 + e * 4 + q - 1, e, q - 1, base + n - 1)
                finish_group(i * 8 + e * 4 + 3, e, 3, base + NI - 1)

            with act.Fori(0, 3) as i:
                act.wait_ge(gate_ld, loaded(i))
                act.activation(gate[:], gate[:], ACT.Sigmoid).then_inc(gate_ok, 1)
                load_ln_exp_tables(nc, act)
                head(i, 0)
                head(i, 1)

        @blk.vector
        def _(dve):
            dve.sem_inc(r_ok, 2)
            dve.sem_inc(fin_ok, 2)
            dve.sem_inc(o_st, 16)
            dve.sem_inc(o_ok, 1)
            for e in both:
                dve.memset(f32(X[e][HD:68, :]), 1.0).then_inc(setup, 1)
                dve.memset(f32(Y[e][HD:68, :]), 1.0).then_inc(setup, 1)
                dve.memset(f32(Z[e][HD:68, :]), 1.0).then_inc(setup, 1)
                dve.memset(V[e][:, :, HD - HD * e:P - HD * e], 1.0).then_inc(setup, 1)
            dve.memset(mx[:], NEG).then_inc(setup, 1)
            dve.wait_ge(consts, 48)
            dve.tensor_copy(ident_b[:], ident[:]).then_inc(setup, 1)
            dve.tensor_copy(mask_b[:], mask[:]).then_inc(setup, 1)
            dve.tensor_copy(maskT_b[:], maskT[:]).then_inc(setup, 1)
            dve.wait_ge(setup, 12)

            def chunk_max(h, m):
                t, c, lo_, hi_ = chunks[m]
                dve.wait_ge(c_ok, h * NCH + m + 1)
                dve.tensor_reduce(mx[:, t, c:c + 1], s1[m % 2][:, 0:hi_ - lo_], AX.X, ALU.max).then_inc(r_ok, 1)

            def head_max(h, first=False):
                dve.wait_ge(r_ok, h * NCH + NCH + 2)
                dve.tensor_reduce(m1[:], mx[:], AX.X, ALU.max).then_inc(m_step, 1)
                dve.wait_ge(m_step, h * 3 + 1)
                dve.tensor_scalar(m_hl[:, 0, :], m1[:], -1.0, None, ALU.mult).then_inc(m_step, 1)
                dve.wait_ge(m_step, h * 3 + 2)
                dve.scalar_tensor_tensor(out=m_hl[:, 1, :], in0=m1[:], scalar=-1.0, in1=f32(m_hl[:, 0, :]),
                                         op0=ALU.mult, op1=ALU.subtract).then_inc(m_step, 1)
                dve.wait_ge(mt_ok, h + 1)
                if not first:
                    dve.wait_ge(m_st, h * 16)
                dve.tensor_copy(m_row[:], s1[0][0:2 * NT, 0:P]).then_inc(mrow_ok, 1)

            def finish_group(i, e, q):
                rows, n4 = slice(HD * e, HD * e + HD), i * 8 + e * 4 + q
                cols = slice(q * 512, (q + 1) * 512)
                if q == 0:
                    if e == 0:
                        dve.wait_ge(gate_ok, i + 1)
                        dve.wait_ge(o_st, loaded(i))
                dve.wait_ge(rd_ok, n4 + 1)
                dve.tensor_tensor(o[rows, cols], acc[q % 2][rows, :], rden[rows, q % 2, :], ALU.mult).then_inc(fin_ok, 1)
                dve.wait_ge(fin_ok, n4 + 3)
                dve.tensor_tensor(o[rows, cols], o[rows, cols], gate[rows, cols], ALU.mult).then_inc(o_ok, 1)

            def head(i, e, last):
                for n, (q, _, _) in enumerate(items):
                    if not last:
                        for m in range((n - FIRST_CHUNK) * PER_ITEM, (n - FIRST_CHUNK + 1) * PER_ITEM):
                            if 0 <= m < NCH:
                                chunk_max(i * 2 + e + 1, m)
                            if m == NCH - 1:
                                head_max(i * 2 + e + 1)
                    if n >= 2 and items[n - 2][0] != items[n - 1][0]:
                        finish_group(i, e, items[n - 2][0])
                finish_group(i, e, 3)

            for m in range(NCH):
                chunk_max(0, m)
            head_max(0, first=True)
            with dve.Fori(0, 2) as i:
                head(i, 0, False)
                head(i, 1, False)
            head(2, 0, False)
            head(2, 1, True)

        @blk.tensor
        def _(pe):
            pe.wait_ge(consts, 48)
            pe.wait_ge(setup, 12)

            def chunk(h, i, e, m, first=False):
                t, c, lo_, hi_ = chunks[m]
                if m == 0:
                    pe.wait_ge(xy_ld[e], i * 48 + 48)
                pe.wait_ge(r_ok, h * NCH + m + 1)
                if m == 0 and not first:
                    pe.wait_ge(mrow_ok, h)
                diag = hi_ == (t + 1) * P
                out = s1[m % 2]
                mm = pe.matmul(out[:, 0:hi_ - lo_], X[e][0:66, t * P:(t + 1) * P], Y[e][0:66, lo_:hi_],
                               start=True, stop=not diag)
                if diag:
                    mm = pe.matmul(out[:, hi_ - lo_ - P:hi_ - lo_], ident_b[:], mask_b[:], start=False, stop=True)
                mm.then_inc(c_ok, 1)

            def max_rows(h):
                pe.wait_ge(m_step, h * 3 + 3)
                pe.transpose(s1[0][0:2 * NT, 0:P], f32(m_hl[:]).rearrange("p a n -> p (a n)"), ident[:]).then_inc(mt_ok, 1)

            def logits(i, e, n):
                q, tiles, off = items[n]
                if n == 0:
                    pe.wait_ge(kq_ld[e], i * 96 + 96)
                    pe.wait_ge(m_ld[e], loaded(i))
                cols = slice(q * 512 + off, (q + 1) * 512)
                for a, j in enumerate(tiles):
                    out = sS[n % 2][:, a, off:512]
                    rows = slice(j * P, (j + 1) * P)
                    diag = j >= 4 * q
                    pe.matmul(out, K1[e][:, rows], Q1[e][:, cols], start=True, stop=False)
                    mm = pe.matmul(out, Y[e][:, rows], Z[e][:, cols], start=False, stop=not diag)
                    if diag:
                        mm = pe.matmul(sS[n % 2][:, a, off:off + P], ident_b[:], maskT_b[:], start=False, stop=True)
                mm.then_inc(s_ok, 1)

            def values(i, e, n):
                q, tiles, off = items[n]
                pe.wait_ge(p_ok, i * (2 * NI) + e * NI + n + 1)
                if tiles[0] == 0:
                    pe.wait_ge(fin_ok, i * 8 + e * 4 + q + 1)
                for a, j in enumerate(tiles):
                    mm = pe.matmul(acc[q % 2][:, off:512], V[e][:, j, :], p[:, n % 2, a, off:512],
                                   start=(j == 0), stop=(j == 4 * q + 3))
                mm.then_inc(pv_ok, 1)

            def head(i, e, last):
                if e == 0:
                    logits(i, e, 0)
                for n in range(NI):
                    if n + 1 < NI:
                        logits(i, e, n + 1)
                    elif e == 0:
                        logits(i, 1, 0)
                    values(i, e, n)
                    if not last:
                        for m in range((n - FIRST_CHUNK) * PER_ITEM, (n - FIRST_CHUNK + 1) * PER_ITEM):
                            if 0 <= m < NCH:
                                chunk(i * 2 + e + 1, i + e, 1 - e, m)
                            if m == NCH - 1:
                                max_rows(i * 2 + e + 1)

            for m in range(NCH):
                chunk(0, 0, 0, m, first=True)
            max_rows(0)
            with pe.Fori(0, 2) as i:
                head(i, 0, False)
                head(i, 1, False)
            head(2, 0, False)
            head(2, 1, True)


def hgrn_mixer(nc, g, hT_hi, hT_lo):
    NJ = len(LEVELS) + 1
    with ExitStack() as ctx:
        sb, ps, sem = maker(nc, ctx, "hg")
        two = range(2)
        w_raw = sb("w_raw", [P, KB, P])
        w_hi, w_lo = sb("w_hi", [P, 2, KB, P], F32R), sb("w_lo", [P, 2, KB, P], F32R)
        stage = sb("stage", [P, 2, 512])
        z, q, gt = (sb(n, [P, 2, NA, P]) for n in ("z", "q", "gt"))
        v = sb("v", [P, 2, NA * P])
        ez, s, f, cum = (sb(n, [P, NA, P]) for n in ("ez", "s", "f", "cum"))
        k = sb("k", [P, NA, P])
        dl, fac = sb("dl", [P, 2, NA, P]), sb("fac", [P, 2, NA, P])
        ex = dl
        ecum, qp = sb("ecum", [P, 2, NA, P]), sb("qp", [P, 2, NA, P])
        kp, kT = sb("kp", [P, NA, P]), sb("kT", [P, 2, NA, P])
        ST = [sb(f"ST{b}", [P, 2 * NA, P]) for b in two]
        St = sb("St", [P, NA, P])
        osq = sb("osq", [P, NA, P])
        r = osq
        o1 = sb("o1", [P, 2, NA, P])
        level, diag = sb("level", [P, len(LEVELS), HD], I32), sb("diag", [P, P], I32)
        ident, headsum = sb("ident", [P, P]), sb("headsum", [P, P])
        gain, lb, one_lb, ones = sb("gain", [P, NA]), sb("lb", [P, NA]), sb("one_lb", [P, NA]), sb("ones", [P, P])
        eps, one, hold = sb("eps", [P, 1]), sb("one", [P, 1]), sb("hold", [P, NJ])
        sc = [[ps(f"sc{b}{e}", [P, NA, P]) for e in two] for b in two]
        ktn_ps, o_ps = ps("ktn", [P, NA, P]), ps("o", [P, NA, P])
        kt_ps = u_ps = n_ps = ktn_ps
        acc = [ps(f"acc{b}", [P, 512]) for b in two]
        ld, v_ld = [sem(f"ld{b}") for b in two], [sem(f"v_ld{b}") for b in two]
        w_ld, stored = sem("w_ld"), [sem(f"stored{b}") for b in two]
        whi_ok, wlo_ok, pm_ok, pev_ok = (sem(n) for n in ("whi_ok", "wlo_ok", "pm_ok", "pev_ok"))
        consts, setup, st = sem("consts"), sem("setup"), [sem(f"st{b}") for b in two]
        (zc_ok, ez_ok, sp_ok, s_ok, f_ok, lf_ok, k_ok, cum_ok, ecum_ok, gt_ok, qp_ok) = (sem(n) for n in (
            "zc_ok", "ez_ok", "sp_ok", "s_ok", "f_ok", "lf_ok", "k_ok", "cum_ok", "ecum_ok", "gt_ok", "qp_ok"))
        dl_ok, ex_ok, fac_ok, sc_ok, put_ok = (sem(n) for n in ("dl_ok", "ex_ok", "fac_ok", "sc_ok", "put_ok"))
        (ktp_ok, kT_ok, o_ok, u_ok, S_ok, osq_ok, n_ok, lnr_ok, r_ok, o1_ok, o2_ok) = (sem(n) for n in (
            "ktp_ok", "kT_ok", "o_ok", "u_ok", "S_ok", "osq_ok", "n_ok", "lnr_ok", "r_ok", "o1_ok", "o2_ok"))
        blk = ctx.enter_context(nc.Block())

        @blk.sync
        def _(sp):
            for t, n in ((level, "c_level"), (diag, "c_diag"), (ident, "c_ident"), (headsum, "c_headsum"),
                         (gain, "hgrn_gain"), (lb, "hgrn_lb")):
                sp.dma_start(t[:], g[n]).then_inc(consts, 16)

            def load_gates(c, b, i):
                if later(c, 2):
                    sp.wait_ge(put_ok, c * NJ - NJ + 2)
                for t, n in ((z, AF), (q, AQ)):
                    sp.dma_start(t[:, b], g["projT"][n:n + NA, :, bass.ds(c * P, P)].rearrange("a p t -> p a t")).then_inc(ld[b], 16)

            def load_values(c, b, i):
                if later(c, 2):
                    sp.wait_ge(o2_ok, c - 1)
                sp.dma_start(gt[:, b], g["projT"][AG:AG + NA, :, bass.ds(c * P, P)].rearrange("a p t -> p a t")).then_inc(v_ld[b], 16)
                sp.dma_start(v[:, b, :], g["v_tok"][bass.ds(c * P, P), 384:768]).then_inc(v_ld[b], 16)

            def store(c, b, i):
                sp.wait_ge(o2_ok, c + 1)
                sp.dma_start(g["mixT"][0:NA, :, bass.ds(c * P, P)].rearrange("a p t -> p a t"), o1[:, b]).then_inc(st[b], 16)

            def weights(c):
                if later(c, 1):
                    sp.wait_ge(wlo_ok, c)
                sp.dma_start(w_raw[:], g["w_blk"][c + NFIRST]).then_inc(w_ld, 16)

            def pair(i, last=False):
                weights(i * 2 + 3)
                load_gates(i * 2 + 3, 1, i + 1)
                load_values(i * 2 + 2, 0, i + 1)
                store(i * 2, 0, i)
                if not last:
                    weights(i * 2 + 4)
                    load_gates(i * 2 + 4, 0, i + 2)
                load_values(i * 2 + 3, 1, i + 1)
                store(i * 2 + 1, 1, i)

            for c in two:
                load_gates(c, c, 0)
                weights(c)
                load_values(c, c, 0)
            weights(2)
            load_gates(2, 0, 1)
            with sp.Fori(0, NT // 2 - 2) as i:
                pair(i)
            pair(NT // 2 - 2, last=True)
            store(NT - 2, 0, 0)
            store(NT - 1, 1, 0)
            for b in two:
                sp.wait_ge(st[b], loaded(NT // 2))

        @blk.scalar
        def _(act):
            load_ln_exp_tables(nc, act)
            act.wait_ge(setup, 6)

            def split_hi(c, b):
                act.wait_ge(w_ld, c * 16 + 16)
                if later(c, 2):
                    act.wait_ge(pm_ok, c * NQ - NQ)
                act.activation(w_hi[:, b], w_raw[:], ACT.Copy).then_inc(whi_ok, 1)

            def evacuate(c, i, b, m):
                act.wait_ge(pm_ok, c * NQ + m + 1)
                act.wait_ge(stored[m % 2], i * 64 + (2 * b + m // 2) * 16 + 16)
                act.activation(stage[:, m % 2, :], acc[m % 2][:], ACT.Copy).then_inc(pev_ok, 1)
                act.wait_ge(pev_ok, done(c * NQ + m))
                act.dma_start(g["projT"][c + NFIRST, :, m * 512:(m + 1) * 512], stage[:, m % 2, :]).then_inc(stored[m % 2], 16)

            split_hi(0, 0)

            def a(c, b, i):
                act.wait_ge(zc_ok, c + 1)
                act.activation(ez[:], z[:, b], ACT.Exp, scale=-1.0).then_inc(ez_ok, 1)
                act.wait_ge(ez_ok, c + 1)
                act.activation(s[:], ez[:], ACT.Ln, bias=one[:, 0:1]).then_inc(sp_ok, 1)
                act.wait_ge(sp_ok, c + 1)
                act.activation(s[:], s[:], ACT.Exp, scale=-1.0).then_inc(s_ok, 1)
                act.wait_ge(f_ok, c * 2 + 2)
                act.activation(f[:], f[:], ACT.Ln).then_inc(lf_ok, 1)
                if before_last(c):
                    split_hi(c + 1, 1 - b)
                act.wait_ge(cum_ok, c * NA + NA)
                if later(c, 2):
                    act.wait_ge(S_ok, c - 1)
                act.activation(ecum[:, b], cum[:], ACT.Exp).then_inc(ecum_ok, 1)
                for j in range(NJ):
                    act.wait_ge(dl_ok, done(c * NJ + j))
                    if j == 0:
                        act.activation(ex[:, 0], dl[:, 0], ACT.Exp, scale=-1.0).then_inc(ex_ok, 1)
                        continue
                    h = LEVELS[j - 1]
                    src = dl[:, j % 2].rearrange("p a (n x h) -> p (a n) x h", x=2, h=h)
                    dst = ex[:, j % 2].rearrange("p a (n x h) -> p (a n) x h", x=2, h=h)
                    act.activation(dst[:, :, 0, :], src[:, :, 0, :], ACT.Exp, scale=-1.0)
                    act.activation(dst[:, :, 1, :], src[:, :, 1, :], ACT.Exp).then_inc(ex_ok, 1)
                    if j in (3, 5, 7):
                        evacuate(c, i, b, (j - 3) // 2)
                act.wait_ge(ktp_ok, c + 1)
                act.activation(kT[:, b], kt_ps[:], ACT.Copy).then_inc(kT_ok, 1)
                evacuate(c, i, b, 3)

            def b_(c, b, i):
                act.wait_ge(o_ok, c + 1)
                act.activation(osq[:], o_ps[:], ACT.Square).then_inc(osq_ok, 1)
                act.wait_ge(n_ok, c + 1)
                act.activation(r[:], n_ps[:], ACT.Ln, scale=1.0 / HD, bias=eps[:, 0:1]).then_inc(lnr_ok, 1)
                act.wait_ge(lnr_ok, c + 1)
                act.activation(r[:], r[:], ACT.Exp, scale=-0.5).then_inc(r_ok, 1)

            over_pairs(act, NT, a, b_)
            for b in two:
                act.wait_ge(stored[b], 16 + NT * NQ // 2 * 16)

        @blk.vector
        def _(dve):
            for ring in (dl_ok, ex_ok, fac_ok, sc_ok, put_ok, pev_ok):
                dve.sem_inc(ring, 2)
            for b in two:
                dve.sem_inc(stored[b], 16)
                dve.sem_inc(st[b], 16)
            for t, val in ((ST[0], 0.0), (ST[1], 0.0), (St, 0.0), (eps, EPS), (one, 1.0), (ones, 1.0)):
                dve.memset(t[:], val).then_inc(setup, 1)
            dve.wait_ge(consts, 96)
            dve.wait_ge(setup, 6)
            dve.tensor_tensor(one_lb[:], lb[:], lb[:], ALU.subtract).then_inc(setup, 1)
            dve.wait_ge(setup, 7)
            dve.tensor_scalar(one_lb[:], one_lb[:], 1.0, None, ALU.add).then_inc(setup, 1)
            dve.wait_ge(setup, 8)
            dve.tensor_tensor(lb[:], one_lb[:], one_lb[:], ALU.subtract).then_inc(setup, 1)
            dve.wait_ge(setup, 9)
            dve.tensor_scalar(one_lb[:], lb[:], -1.0, 1.0, ALU.mult, ALU.add).then_inc(setup, 1)
            dve.wait_ge(setup, 10)

            def bc(t):
                return t.unsqueeze(2).broadcast_to([P, NA, P])

            def split_lo(c, b):
                dve.wait_ge(whi_ok, c + 1)
                dve.tensor_tensor(w_lo[:, b], w_raw[:], f32(w_hi[:, b]), ALU.subtract).then_inc(wlo_ok, 1)

            split_lo(0, 0)

            def a(c, b, i):
                dve.wait_ge(ld[b], i * 32 + 32)
                dve.tensor_scalar(z[:, b], z[:, b], -44.0, None, ALU.max).then_inc(zc_ok, 1)
                dve.wait_ge(s_ok, c + 1)
                for m in range(NA):
                    op = dve.tensor_scalar(f[:, m, :], s[:, m, :], one_lb[:, m:m + 1], lb[:, m:m + 1], ALU.mult, ALU.add)
                op.then_inc(f_ok, 1)
                dve.wait_ge(f_ok, c * 2 + 1)
                dve.tensor_scalar(f[:], f[:], MIN_FORGET, None, ALU.max).then_inc(f_ok, 1)
                dve.tensor_tensor(k[:], ez[:], s[:], ALU.mult).then_inc(k_ok, 1)
                dve.wait_ge(k_ok, c * 2 + 1)
                dve.tensor_tensor(k[:], k[:], bc(one_lb[:]), ALU.mult).then_inc(k_ok, 1)
                dve.wait_ge(lf_ok, c + 1)
                for m in range(NA):
                    dve.tensor_tensor_scan(cum[:, m, :], ones[:], f[:, m, :], 0.0, ALU.mult, ALU.add).then_inc(cum_ok, 1)
                dve.wait_ge(cum_ok, c * NA + NA)
                dve.wait_ge(k_ok, c * 2 + 2)

                if before_last(c):
                    split_lo(c + 1, 1 - b)

                def diff(j):
                    dve.wait_ge(fac_ok, free(c * NJ + j))
                    if j == 0:
                        dve.tensor_tensor(dl[:, 0], cum[:], cum[:, :, P - 1:P].broadcast_to([P, NA, P]),
                                          ALU.subtract).then_inc(dl_ok, 1)
                        return
                    h = LEVELS[j - 1]
                    cv = cum[:].rearrange("p a (n x) -> p (a n) x", x=2 * h)
                    ref = cv[:, :, h - 1:h].broadcast_to([P, NA * (HD // h), 2 * h])
                    dve.tensor_tensor(dl[:, j % 2].rearrange("p a (n x) -> p (a n) x", x=2 * h), cv, ref,
                                      ALU.subtract).then_inc(dl_ok, 1)

                def factors(j):
                    dve.wait_ge(ex_ok, done(c * NJ + j))
                    if j == 0:
                        if later(c, 1):
                            dve.wait_ge(ktp_ok, c)
                        dve.tensor_tensor(kp[:], k[:], ex[:, 0], ALU.mult).then_inc(fac_ok, 1)
                        return
                    dve.wait_ge(sc_ok, free(c * NJ + j))
                    h = LEVELS[j - 1]
                    view = lambda t: t.rearrange("p a (n x h) -> p (a n) x h", x=2, h=h)
                    dst, e = view(fac[:, j % 2]), view(ex[:, j % 2])
                    dve.tensor_tensor(dst[:, :, 0, :], view(k[:])[:, :, 0, :], e[:, :, 0, :], ALU.mult)
                    dve.tensor_tensor(dst[:, :, 1, :], view(q[:, b])[:, :, 1, :], e[:, :, 1, :], ALU.mult).then_inc(fac_ok, 1)

                def put(j):
                    dve.wait_ge(sc_ok, done(c * NJ + j))
                    if j == 0 and later(c, 2):
                        dve.wait_ge(o_ok, c - 1)
                    dve.wait_ge(put_ok, c * NJ + j + 2)
                    dve.memset(hold[:, j:j + 1], 0.0)
                    for e in two:
                        dst = ST[b][:].rearrange("p (a e) t -> p a e t", e=2)[:, :, e, :]
                        src = sc[j % 2][e]
                        if j == 0:
                            m = diag[:].unsqueeze(1).broadcast_to([P, NA, P])
                            op = dve.copy_predicated(dst, m, src[:])
                        else:
                            h = LEVELS[j - 1]
                            m = level[:, j - 1, :].rearrange("p (n h) -> p n h", h=h)
                            for a_ in range(NA):
                                op = dve.copy_predicated(
                                    dst[:, a_].rearrange("p (n x h) -> p n x h", x=2, h=h)[:, :, 1, :], m,
                                    src[:, a_, 0:HD].rearrange("p (n h) -> p n h", h=h))
                    op.then_inc(put_ok, 1)

                diff(0)
                diff(1)
                for j in range(NJ):
                    factors(j)
                    if j + 2 < NJ:
                        diff(j + 2)
                    if j == 1:
                        dve.wait_ge(ecum_ok, c + 1)
                        dve.tensor_tensor(qp[:, b], q[:, b], ecum[:, b], ALU.mult).then_inc(qp_ok, 1)
                    if j >= 1:
                        put(j - 1)
                put(NJ - 1)

            def b_(c, b, i):
                dve.wait_ge(v_ld[b], i * 32 + 32)
                dve.tensor_tensor(gt[:, b], gt[:, b], bc(gain[:]), ALU.mult).then_inc(gt_ok, 1)
                dve.wait_ge(u_ok, c + 1)
                for m in range(NA):
                    for e in two:
                        rows = slice(HD * e, HD * e + HD)
                        op = dve.scalar_tensor_tensor(out=St[rows, m, rows], in0=St[rows, m, rows],
                                                      scalar=ecum[rows, b, m, P - 1:P], in1=u_ps[rows, m, rows],
                                                      op0=ALU.mult, op1=ALU.add)
                op.then_inc(S_ok, 1)
                dve.wait_ge(r_ok, c + 1)
                dve.wait_ge(st[b], loaded(i))
                dve.tensor_tensor(o1[:, b], o_ps[:], r[:], ALU.mult).then_inc(o1_ok, 1)
                dve.wait_ge(o1_ok, c + 1)
                dve.wait_ge(gt_ok, c + 1)
                dve.tensor_tensor(o1[:, b], o1[:, b], gt[:, b], ALU.mult).then_inc(o2_ok, 1)

            over_pairs(dve, NT, a, b_)

        @blk.tensor
        def _(pe):
            pe.wait_ge(consts, 96)
            pe.wait_ge(setup, 6)

            def piece(c, b, j):
                m = j // 2
                if j == 0:
                    pe.wait_ge(wlo_ok, c + 1)
                if j % 2 == 0:
                    pe.wait_ge(pev_ok, free(c * NQ + m))
                cols = slice(m * 512, (m + 1) * 512)
                for k_ in range(j % 2 * (KB // 2), (j % 2 + 1) * (KB // 2)):
                    mm = three_passes(pe, acc[m % 2][:], w_hi[:, b, k_], w_lo[:, b, k_],
                                      hT_hi[:, k_, cols], hT_lo[:, k_, cols], k_ == 0, k_ == KB - 1)
                if j % 2:
                    mm.then_inc(pm_ok, 1)

            def a(c, b, i):
                pe.wait_ge(fac_ok, c * NJ + 3)
                if later(c, 2):
                    pe.wait_ge(lnr_ok, c - 1)
                for m in range(NA):
                    mm = pe.transpose(kt_ps[:, m, :], kp[:, m, :], ident[:])
                mm.then_inc(ktp_ok, 1)
                for j in range(NJ):
                    pe.wait_ge(fac_ok, done(c * NJ + j))
                    pe.wait_ge(put_ok, free(c * NJ + j))
                    for e in two:
                        rows = slice(HD * e, HD * e + HD)
                        for m in range(NA):
                            if j == 0:
                                mm = pe.matmul(sc[0][e][:, m, :], k[rows, m, :], q[rows, b, m, :], start=True, stop=True)
                            else:
                                h = LEVELS[j - 1]
                                right = fac[rows, j % 2, m, :].rearrange("p (n x h) -> p n x h", x=2, h=h)[:, :, 1, :]
                                mm = pe.matmul(sc[j % 2][e][:, m, 0:HD].rearrange("p (n h) -> p n h", h=h), fac[rows, j % 2, m, :], right,
                                               start=True, stop=True)
                    mm.then_inc(sc_ok, 1)
                    piece(c, b, j)

            def b_(c, b, i):
                pe.wait_ge(put_ok, c * NJ + NJ + 2)
                pe.wait_ge(qp_ok, c + 1)
                pe.wait_ge(v_ld[b], i * 32 + 32)
                if later(c, 1):
                    pe.wait_ge(S_ok, c)
                    pe.wait_ge(o1_ok, c)
                for m in range(NA):
                    pe.matmul(o_ps[:, m, :], St[:, m, :], qp[:, b, m, :], start=True, stop=False)
                    for e in two:
                        rows = slice(HD * e, HD * e + HD)
                        mm = pe.matmul(o_ps[rows, m, :], v[:, b, m * P + HD * e:m * P + HD * e + HD], ST[b][:, 2 * m + e, :],
                                       start=False, stop=True)
                mm.then_inc(o_ok, 1)
                pe.wait_ge(kT_ok, c + 2 if before_last(c) else c + 1)
                for m in range(NA):
                    mm = pe.matmul(u_ps[:, m, :], kT[:, b, m, :], v[:, b, m * P:(m + 1) * P], start=True, stop=True)
                mm.then_inc(u_ok, 1)
                pe.wait_ge(osq_ok, c + 1)
                pe.wait_ge(S_ok, c + 1)
                mm = pe.matmul(n_ps[:].rearrange("p a t -> p (a t)"), headsum[:], osq[:].rearrange("p a t -> p (a t)"),
                               start=True, stop=True)
                mm.then_inc(n_ok, 1)

            over_pairs(pe, NT, a, b_)


def retention_and_output(nc, g):
    VW = 4 * HD
    with ExitStack() as ctx:
        sb, ps, sem = maker(nc, ctx, "ro")
        two = range(2)
        xq, xk = sb("xq", [P, 2, NC, P]), sb("xk", [P, 2, NC, P])
        gt = sb("gt", [P, NC, T])
        v, cs = sb("v", [P, 2, VW]), sb("cs", [P, 2, 2, P])
        xc, xs = sb("xc", [P, 2, NC, P]), sb("xs", [P, 2, NC, P])
        rot = sb("rot", [P, 2, 2, NC, P])
        qm = sb("qm", [P, 4, NC, P])
        qs, ks, kT = sb("qs", [P, 2, NC, P]), sb("ks", [P, NC, P]), sb("kT", [P, 2, NC, P])
        ST = [sb(f"ST{b}", [P, 4, P]) for b in two]
        Rst, um = sb("Rst", [P, NC, VW]), sb("um", [P, NC, VW])
        osq, r, o1 = sb("osq", [P, NC, P]), sb("r", [P, NC, P]), sb("o1", [P, NC, P])
        intra, own, hmask = sb("intra", [P, 4, P]), sb("own", [P, VW]), sb("hmask", [P, 4])
        qscale, kscale, decay = sb("qscale", [P, P]), sb("kscale", [P, P]), sb("decay", [P, 1])
        ident, headsum, rgain, eps = sb("ident", [P, P]), sb("headsum", [P, P]), sb("rgain", [P, NC]), sb("eps", [P, 1])
        w_raw = sb("w_raw", [P, 2, D])
        w_hi, w_lo = sb("w_hi", [P, KB, D], F32R), sb("w_lo", [P, KB, D], F32R)
        m_raw = sb("m_raw", [P, 2, KB, P])
        m_hi, m_lo = sb("m_hi", [P, 2, KB, P], F32R), sb("m_lo", [P, 2, KB, P], F32R)
        x, y, junk = sb("x", [P, 2, D]), sb("y", [P, 2, D]), sb("junk", [P, D])
        gain, rs = sb("gain", [P, D]), sb("rs", [P, 2, 4])
        sc, kt_ps, u_ps, o_ps = ps("sc", [P, 4, P]), ps("ktn", [P, NC, P]), ps("u", [P, NC, VW]), ps("o", [P, NC, P])
        n_ps = kt_ps
        acc = [ps(f"acc{b}", [P, 2, 512]) for b in two]
        w_ld, m_ld, x_ld, ld, st = ([sem(f"{n}{b}") for b in two] for n in ("w_ld", "m_ld", "x_ld", "ld", "st"))
        consts, setup, gt_ld, silu_ok = sem("consts"), sem("setup"), sem("gt_ld"), sem("silu_ok")
        (xcs_ok, rot_ok, qm_ok, qs_ok, ks_ok, sc_ok, st_ok, ktp_ok, kT_ok, o_ok, u_ok, um_ok, R_ok) = (
            sem(n) for n in ("xcs_ok", "rot_ok", "qm_ok", "qs_ok", "ks_ok", "sc_ok", "st_ok", "ktp_ok",
                             "kT_ok", "o_ok", "u_ok", "um_ok", "R_ok"))
        osq_ok, n_ok, lnr_ok, r_ok, o1_ok, o2_ok = (sem(n) for n in ("osq_ok", "n_ok", "lnr_ok", "r_ok", "o1_ok", "o2_ok"))
        whi_ok, wlo_ok, mhi_ok, mlo_ok, mm_ok, sq_ok, ln_ok, rs_ok, y_ok, x_ok = (sem(n) for n in (
            "whi_ok", "wlo_ok", "mhi_ok", "mlo_ok", "mm_ok", "sq_ok", "ln_ok", "rs_ok", "y_ok", "x_ok"))
        blk = ctx.enter_context(nc.Block())

        @blk.sync
        def _(sp):
            sp.dma_start(gt[:], g["projT"][CG:CG + NC].rearrange("a p t -> p a t")).then_inc(gt_ld, 16)
            for t, n in ((intra, "c_intra"), (own, "c_own"), (qscale, "c_qscale"), (kscale, "c_kscale"), (hmask, "c_hmask"),
                         (decay, "c_cdecay"), (ident, "c_ident"), (headsum, "c_headsum"), (rgain, "ret_gain")):
                sp.dma_start(t[:], g[n]).then_inc(consts, 16)
            sp.dma_start(gain[:], g["g_mix_post"][0:1, :].broadcast_to([P, D])).then_inc(consts, 16)

            def load(c, b, i):
                cols = bass.ds(c * P, P)
                if later(c, 2):
                    sp.wait_ge(o2_ok, c - 1)
                for t, n in ((xq, CQ), (xk, CK)):
                    sp.dma_start(t[:, b], g["projT"][n:n + NC, :, cols].rearrange("a p t -> p a t")).then_inc(ld[b], 16)
                sp.dma_start(cs[:, b, 0, :], g["c_cos"][:, cols]).then_inc(ld[b], 16)
                sp.dma_start(cs[:, b, 1, :], g["c_sin"][:, cols]).then_inc(ld[b], 16)
                sp.dma_start(v[:, b, :], g["v_tok"][cols, 768:1024]).then_inc(ld[b], 16)

            def load_mixed(c, b, i):
                cols = bass.ds(c * P, P)
                if later(c, 2):
                    sp.wait_ge(x_ok, c - 1)
                sp.dma_start(m_raw[:, b, 0:6], g["mixT"][0:6, :, cols].rearrange("k p t -> p k t")).then_inc(m_ld[b], 16)
                sp.dma_start(x[:, b, :], g["x"][cols, :]).then_inc(x_ld[b], 16)

            load(0, 0, 0)
            load(1, 1, 0)
            for k in range(KB):
                if k >= 2:
                    sp.wait_ge(wlo_ok, k - 1)
                sp.dma_start(w_raw[:, k % 2, :], g["w_out"][k]).then_inc(w_ld[k % 2], 16)
            load_mixed(0, 0, 0)
            load_mixed(1, 1, 0)
            with sp.Fori(0, NT // 2 - 1) as i:
                load(i * 2 + 2, 0, i + 1)
                load(i * 2 + 3, 1, i + 1)
                load_mixed(i * 2 + 2, 0, i + 1)
                load_mixed(i * 2 + 3, 1, i + 1)

        @blk.scalar
        def _(act):
            act.wait_ge(gt_ld, 16)
            act.activation(gt[:], gt[:], ACT.Silu).then_inc(silu_ok, 1)
            load_ln_exp_tables(nc, act)
            act.wait_ge(setup, 2)
            for k in range(KB):
                act.wait_ge(w_ld[k % 2], 16 * (k // 2) + 16)
                act.activation(w_hi[:, k, :], w_raw[:, k % 2, :], ACT.Copy).then_inc(whi_ok, 1)

            def a(c, b, i):
                act.wait_ge(ktp_ok, c + 1)
                act.activation(kT[:, b], kt_ps[:], ACT.Copy).then_inc(kT_ok, 1)

            def b_(c, b, i):
                act.wait_ge(o_ok, c + 1)
                act.activation(osq[:], o_ps[:], ACT.Square).then_inc(osq_ok, 1)
                act.wait_ge(n_ok, c + 1)
                act.activation(r[:], n_ps[:], ACT.Ln, scale=1.0 / HD, bias=eps[:, 0:1]).then_inc(lnr_ok, 1)
                act.wait_ge(lnr_ok, c + 1)
                act.activation(r[:], r[:], ACT.Exp, scale=-0.5).then_inc(r_ok, 1)
                act.wait_ge(m_ld[b], loaded(i))
                act.wait_ge(o2_ok, c + 1)
                act.wait_ge(mm_ok, free(c))
                act.activation(m_hi[:, b], m_raw[:, b], ACT.Copy).then_inc(mhi_ok, 1)

            def o(n, b, i):
                act.wait_ge(mm_ok, done(n))
                act.wait_ge(y_ok, free(n))
                act.activation(junk[:], acc[b][:].rearrange("p a n -> p (a n)"), ACT.Square,
                               accum_out=rs[:, b, 0:1]).then_inc(sq_ok, 1)
                act.wait_ge(sq_ok, n + 1)
                act.activation(rs[:, b, 1:2], rs[:, b, 0:1], ACT.Ln, scale=1.0 / D, bias=eps[:, 0:1]).then_inc(ln_ok, 1)
                act.wait_ge(ln_ok, n + 1)
                act.activation(rs[:, b, 2:3], rs[:, b, 1:2], ACT.Exp, scale=-0.5).then_inc(rs_ok, 1)
                act.wait_ge(x_ok, n + 1)
                act.dma_start(g["x_mid"][bass.ds(n * P, P), :], y[:, b, :]).then_inc(st[b], 16)

            over_three(act, NT, a, b_, o)
            for b in two:
                act.wait_ge(st[b], loaded(NT // 2))

        @blk.vector
        def _(dve):
            for ring in (mlo_ok, mm_ok, y_ok):
                dve.sem_inc(ring, 2)
            for b in two:
                dve.sem_inc(st[b], 16)
            dve.memset(Rst[:], 0.0).then_inc(setup, 1)
            dve.memset(eps[:], EPS).then_inc(setup, 1)
            dve.wait_ge(consts, 160)
            dve.wait_ge(silu_ok, 1)
            for m in range(NC):
                dve.tensor_scalar(gt[:, m, :], gt[:, m, :], rgain[:, m:m + 1], None, ALU.mult).then_inc(setup, 1)
            dve.wait_ge(setup, 4)
            for k in range(KB):
                dve.wait_ge(whi_ok, k + 1)
                dve.tensor_tensor(w_lo[:, k, :], w_raw[:, k % 2, :], f32(w_hi[:, k, :]), ALU.subtract).then_inc(wlo_ok, 1)

            def bc(t):
                return t.unsqueeze(1).broadcast_to([P, NC, P])

            def a(c, b, i):
                dve.wait_ge(ld[b], i * 80 + 80)
                for m, t in enumerate((xq, xk)):
                    dve.tensor_tensor(xc[:, m], t[:, b], bc(cs[:, b, 0, :]), ALU.mult)
                    dve.tensor_tensor(xs[:, m], t[:, b], bc(cs[:, b, 1, :]), ALU.mult).then_inc(xcs_ok, 1)
                dve.wait_ge(xcs_ok, c * 2 + 2)
                dve.tensor_tensor(rot[:, b, :, 0, :], xc[:, :, 0, :], xs[:, :, 1, :], ALU.subtract)
                dve.tensor_tensor(rot[:, b, :, 1, :], xs[:, :, 0, :], xc[:, :, 1, :], ALU.add).then_inc(rot_ok, 1)
                dve.wait_ge(rot_ok, c + 1)
                for h in range(4):
                    op = dve.tensor_scalar(qm[:, h], rot[:, b, 0], hmask[:, h:h + 1], None, ALU.mult)
                op.then_inc(qm_ok, 1)
                dve.tensor_tensor(qs[:, b], rot[:, b, 0], bc(qscale[:]), ALU.mult).then_inc(qs_ok, 1)
                if later(c, 1):
                    dve.wait_ge(ktp_ok, c)
                dve.tensor_tensor(ks[:], rot[:, b, 1], bc(kscale[:]), ALU.mult).then_inc(ks_ok, 1)
                dve.wait_ge(sc_ok, c + 1)
                if later(c, 2):
                    dve.wait_ge(o_ok, c - 1)
                dve.tensor_tensor(ST[b][:], sc[:], intra[:], ALU.mult).then_inc(st_ok, 1)

            def b_(c, b, i):
                dve.wait_ge(u_ok, c + 1)
                dve.tensor_tensor(um[:], u_ps[:], own[:].unsqueeze(1).broadcast_to([P, NC, VW]), ALU.mult).then_inc(um_ok, 1)
                dve.wait_ge(um_ok, c + 1)
                dve.scalar_tensor_tensor(out=Rst[:], in0=Rst[:], scalar=decay[:, 0:1], in1=um[:],
                                         op0=ALU.mult, op1=ALU.add).then_inc(R_ok, 1)
                dve.wait_ge(r_ok, c + 1)
                dve.tensor_tensor(o1[:], o_ps[:], r[:], ALU.mult).then_inc(o1_ok, 1)
                dve.wait_ge(o1_ok, c + 1)
                dve.wait_ge(mlo_ok, free(c))
                dve.tensor_tensor(m_raw[:, b, 6:8], o1[:], gt[:, :, bass.ds(c * P, P)], ALU.mult).then_inc(o2_ok, 1)
                dve.wait_ge(mhi_ok, c + 1)
                dve.tensor_tensor(m_lo[:, b], m_raw[:, b], f32(m_hi[:, b]), ALU.subtract).then_inc(mlo_ok, 1)

            def o(n, b, i):
                dve.wait_ge(rs_ok, n + 1)
                dve.wait_ge(st[b], loaded(i))
                dve.scalar_tensor_tensor(out=y[:, b, :], in0=acc[b][:].rearrange("p a n -> p (a n)"),
                                         scalar=rs[:, b, 2:3], in1=gain[:], op0=ALU.mult, op1=ALU.mult).then_inc(y_ok, 1)
                dve.wait_ge(x_ld[b], loaded(i))
                dve.wait_ge(y_ok, done(n))
                dve.tensor_tensor(y[:, b, :], x[:, b, :], y[:, b, :], ALU.add).then_inc(x_ok, 1)

            over_three(dve, NT, a, b_, o)

        @blk.tensor
        def _(pe):
            pe.wait_ge(consts, 160)
            pe.wait_ge(setup, 2)

            def a(c, b, i):
                pe.wait_ge(qm_ok, c + 1)
                if later(c, 1):
                    pe.wait_ge(st_ok, c)
                for h in range(4):
                    for m in range(NC):
                        mm = pe.matmul(sc[:, h, :], rot[:, b, 1, m, :], qm[:, h, m, :], start=(m == 0), stop=(m == NC - 1))
                mm.then_inc(sc_ok, 1)
                pe.wait_ge(ks_ok, c + 1)
                if later(c, 1):
                    pe.wait_ge(kT_ok, c)
                if later(c, 2):
                    pe.wait_ge(lnr_ok, c - 1)
                for m in range(NC):
                    mm = pe.transpose(kt_ps[:, m, :], ks[:, m, :], ident[:])
                mm.then_inc(ktp_ok, 1)

            def b_(c, b, i):
                pe.wait_ge(st_ok, c + 1)
                pe.wait_ge(qs_ok, c + 1)
                if later(c, 1):
                    pe.wait_ge(R_ok, c)
                    pe.wait_ge(o1_ok, c)
                for m in range(NC):
                    for k in range(NC):
                        pe.matmul(o_ps[:, m, :], Rst[:, k, m * P:(m + 1) * P], qs[:, b, k, :], start=(k == 0), stop=False)
                    for e in two:
                        h = 2 * m + e
                        mm = pe.matmul(o_ps[HD * e:HD * e + HD, m, :], v[:, b, HD * h:HD * h + HD], ST[b][:, h, :],
                                       start=False, stop=True)
                mm.then_inc(o_ok, 1)
                pe.wait_ge(kT_ok, c + 2 if before_last(c) else c + 1)
                for m in range(NC):
                    mm = pe.matmul(u_ps[:, m, :], kT[:, b, m, :], v[:, b, :], start=True, stop=True)
                mm.then_inc(u_ok, 1)
                pe.wait_ge(osq_ok, c + 1)
                mm = pe.matmul(n_ps[:].rearrange("p a t -> p (a t)"), headsum[:], osq[:].rearrange("p a t -> p (a t)"),
                               start=True, stop=True)
                mm.then_inc(n_ok, 1)

            def o(n, b, i):
                pe.wait_ge(mlo_ok, done(n))
                pe.wait_ge(y_ok, free(n))
                for c in two:
                    cols = slice(c * 512, (c + 1) * 512)
                    for k in range(KB):
                        mm = three_passes(pe, acc[b][:, c, :], m_hi[:, b, k], m_lo[:, b, k],
                                          w_hi[:, k, cols], w_lo[:, k, cols], k == 0, k == KB - 1)
                mm.then_inc(mm_ok, 1)

            pe.wait_ge(wlo_ok, KB)
            over_three(pe, NT, a, b_, o)


TH = T // 2
MT = TH // P


def mlp(nc, g, half, hT_hi, hT_lo, halo):
    with ExitStack() as ctx:
        sb, ps, sem = maker(nc, ctx, f"ml{half}")
        two = range(2)
        y = sb("y", [P, MT, D])
        w_raw = sb("w_raw", [P, 2, KB, P])
        w_hi, w_lo = sb("w_hi", [P, 2, KB, P], F32R), sb("w_lo", [P, 2, KB, P], F32R)
        d_raw = sb("d_raw", [P, D])
        d_hi, d_lo = sb("d_hi", [P, 2, D], F32R), sb("d_lo", [P, 2, D], F32R)
        conv = sb("conv", [P, FB, 2, 4])
        u, cv = sb("u", [P, 2, TH + 2]), sb("cv", [P, 2, TH])
        ff = sb("ff", [P, TH])
        ff_hi, ff_lo = sb("ff_hi", [P, 2, TH], F32R), sb("ff_lo", [P, 2, TH], F32R)
        gain, eps, rs, x = sb("gain", [P, D]), sb("eps", [P, 1]), sb("rs", [P, 2, 4]), sb("x", [P, 2, D])
        up = [ps(f"up{e}", [P, 2, 512]) for e in two]
        dn = [ps(f"dn{b}", [P, 2, 512]) for b in two]
        consts, y0, setup, d_ld = sem("consts"), sem("y0"), sem("setup"), sem("d_ld")
        w_ld, x_ld, st = ([sem(f"{n}{e}") for e in two] for n in ("w_ld", "x_ld", "st"))
        (whi_ok, wlo_ok, dhi_ok, dlo_ok, up_ok, ev_ok, tap_ok, cv_ok, sg_ok, ff_ok, ffhi_ok, fflo_ok, dn_ok,
         add_ok) = (sem(n) for n in (
             "whi_ok", "wlo_ok", "dhi_ok", "dlo_ok", "up_ok", "ev_ok", "tap_ok", "cv_ok", "sg_ok", "ff_ok",
             "ffhi_ok", "fflo_ok", "dn_ok", "add_ok"))
        sq_ok, ln_ok, r_ok, yn_ok, x_ok = (sem(n) for n in ("sq_ok", "ln_ok", "r_ok", "yn_ok", "x_ok"))
        blk = ctx.enter_context(nc.Block())

        def rows(t):
            return bass.ds(t * P + half * TH, P)

        @blk.gpsimd
        def _(pool):
            pool.memset(y[:], 0.0).then_inc(y0, 1)

        @blk.sync
        def _(sp):
            sp.dma_start(conv[:], g["conv"]).then_inc(consts, 16)
            sp.dma_start(gain[:], g["g_ffn_post"][0:1, :].broadcast_to([P, D])).then_inc(consts, 16)
            with sp.Fori(0, FB) as j:
                for e in two:
                    sp.wait_ge(wlo_ok, free(j * 2 + e))
                    sp.dma_start(w_raw[:, e], g["w_up"][j, e]).then_inc(w_ld[e], 16)
                sp.wait_ge(dlo_ok, j + 1)
                sp.dma_start(d_raw[:], g["w_down"][j]).then_inc(d_ld, 16)
            with sp.Fori(0, MT // 2) as i:
                for b in two:
                    sp.wait_ge(st[b], loaded(i))
                    sp.dma_start(x[:, b, :], g["x_mid"][rows(i * 2 + b), :]).then_inc(x_ld[b], 16)

        @blk.scalar
        def _(act):
            act.wait_ge(consts, 32)
            act.wait_ge(setup, 3)

            def split(j, e):
                act.wait_ge(w_ld[e], j * 16 + 16)
                act.wait_ge(up_ok, free(j * 2 + e))
                act.activation(w_hi[:, e], w_raw[:, e], ACT.Copy).then_inc(whi_ok, 1)

            def evacuate(j, e):
                act.wait_ge(up_ok, done(j * 2 + e))
                pu = up[e][:].rearrange("p a n -> p (a n)")
                if half:
                    act.activation(u[:, e, 0:2], halo[:, j, e, :], ACT.Copy)
                else:
                    act.activation(halo[:, j, e, :], pu[:, TH - 2:TH], ACT.Copy)
                act.activation(u[:, e, 2:TH + 2], pu, ACT.Copy)
                act.activation(cv[:, e, :], pu, ACT.Identity, scale=conv[:, j, e, 2:3],
                               bias=conv[:, j, e, 3:4]).then_inc(ev_ok, 1)

            def hidden(j, b):
                act.wait_ge(d_ld, j * 16 + 16)
                act.wait_ge(dn_ok, j * MT - MT + 2) if later(j, 2) else None
                act.activation(d_hi[:, b, :], d_raw[:], ACT.Copy).then_inc(dhi_ok, 1)
                act.wait_ge(cv_ok, j * 2 + 1)
                act.activation(cv[:, 0, :], cv[:, 0, :], ACT.Silu).then_inc(sg_ok, 1)
                act.wait_ge(ff_ok, j + 1)
                act.activation(ff_hi[:, b, :], ff[:], ACT.Copy).then_inc(ffhi_ok, 1)

            def step(j, b):
                split(j + 1, 0)
                evacuate(j, 0)
                evacuate(j, 1)
                split(j + 1, 1)
                hidden(j, b)

            split(0, 0)
            split(0, 1)
            step(0, 0)
            step(1, 1)
            with act.Fori(1, FB // 2 - 1) as i:
                step(i * 2, 0)
                step(i * 2 + 1, 1)
            step(FB - 2, 0)
            evacuate(FB - 1, 0)
            evacuate(FB - 1, 1)
            hidden(FB - 1, 1)

            load_ln_exp_tables(nc, act)
            act.wait_ge(add_ok, FB * MT + 2)
            with act.Fori(0, MT // 2) as i:
                for b in two:
                    act.wait_ge(yn_ok, free(i * 2 + b))
                    act.activation(ff[:], y[:, i * 2 + b, :], ACT.Square, accum_out=rs[:, b, 0:1]).then_inc(sq_ok, 1)
                    act.wait_ge(sq_ok, i * 2 + b + 1)
                    act.activation(rs[:, b, 1:2], rs[:, b, 0:1], ACT.Ln, scale=1.0 / D, bias=eps[:, 0:1]).then_inc(ln_ok, 1)
                    act.wait_ge(ln_ok, i * 2 + b + 1)
                    act.activation(rs[:, b, 2:3], rs[:, b, 1:2], ACT.Exp, scale=-0.5).then_inc(r_ok, 1)
                    act.wait_ge(x_ok, i * 2 + b + 1)
                    act.dma_start(g["out"][rows(i * 2 + b), :], x[:, b, :]).then_inc(st[b], 16)
            for b in two:
                act.wait_ge(st[b], loaded(MT // 2))

        @blk.vector
        def _(dve):
            for ring in (wlo_ok, up_ok, add_ok, dn_ok, yn_ok):
                dve.sem_inc(ring, 2)
            dve.sem_inc(dlo_ok, 1)
            for b in two:
                dve.sem_inc(st[b], 16)
                dve.memset(u[:, b, 0:2], 0.0).then_inc(setup, 1)
            dve.memset(eps[:], EPS).then_inc(setup, 1)
            dve.wait_ge(consts, 32)
            dve.wait_ge(y0, 1)

            def split(j, e):
                dve.wait_ge(whi_ok, j * 2 + e + 1)
                dve.tensor_tensor(w_lo[:, e], w_raw[:, e], f32(w_hi[:, e]), ALU.subtract).then_inc(wlo_ok, 1)

            def convolve(j, e):
                dve.wait_ge(ev_ok, j * 2 + e + 1)
                dve.scalar_tensor_tensor(out=cv[:, e, :], in0=u[:, e, 1:TH + 1], scalar=conv[:, j, e, 1:2],
                                         in1=cv[:, e, :], op0=ALU.mult, op1=ALU.add).then_inc(tap_ok, 1)
                dve.wait_ge(tap_ok, j * 2 + e + 1)
                dve.scalar_tensor_tensor(out=cv[:, e, :], in0=u[:, e, 0:TH], scalar=conv[:, j, e, 0:1],
                                         in1=cv[:, e, :], op0=ALU.mult, op1=ALU.add).then_inc(cv_ok, 1)

            def add(j, t):
                dve.wait_ge(dn_ok, j * MT + t + 3)
                dve.tensor_tensor(y[:, t, :], y[:, t, :], dn[t % 2][:].rearrange("p a n -> p (a n)"),
                                  ALU.add).then_inc(add_ok, 1)

            def hidden(j, b):
                dve.wait_ge(dhi_ok, j + 1)
                dve.tensor_tensor(d_lo[:, b, :], d_raw[:], f32(d_hi[:, b, :]), ALU.subtract).then_inc(dlo_ok, 1)
                dve.wait_ge(sg_ok, j + 1)
                dve.wait_ge(cv_ok, j * 2 + 2)
                dve.tensor_tensor(ff[:], cv[:, 0, :], cv[:, 1, :], ALU.mult).then_inc(ff_ok, 1)
                dve.wait_ge(ffhi_ok, j + 1)
                dve.tensor_tensor(ff_lo[:, b, :], ff[:], f32(ff_hi[:, b, :]), ALU.subtract).then_inc(fflo_ok, 1)

            def step(j, b, first=False, last=False):
                if not last:
                    split(j + 1, 0)
                if not first:
                    for t in range(MT):
                        add(j - 1, t)
                if not last:
                    split(j + 1, 1)
                convolve(j, 0)
                convolve(j, 1)
                hidden(j, b)

            split(0, 0)
            split(0, 1)
            step(0, 0, first=True)
            step(1, 1)
            with dve.Fori(1, FB // 2 - 1) as i:
                step(i * 2, 0)
                step(i * 2 + 1, 1)
            step(FB - 2, 0)
            step(FB - 1, 1, last=True)
            for t in range(MT):
                add(FB - 1, t)

            with dve.Fori(0, MT // 2) as i:
                for b in two:
                    n = i * 2 + b
                    dve.wait_ge(r_ok, n + 1)
                    dve.scalar_tensor_tensor(out=y[:, n, :], in0=y[:, n, :], scalar=rs[:, b, 2:3], in1=gain[:],
                                             op0=ALU.mult, op1=ALU.mult).then_inc(yn_ok, 1)
                    dve.wait_ge(x_ld[b], loaded(i))
                    dve.wait_ge(yn_ok, done(n))
                    dve.tensor_tensor(x[:, b, :], x[:, b, :], y[:, n, :], ALU.add).then_inc(x_ok, 1)

        @blk.tensor
        def _(pe):
            def project_up(j, b, i):
                for e in two:
                    pe.wait_ge(wlo_ok, done(j * 2 + e))
                    pe.wait_ge(ev_ok, j * 2 + e - 1) if later(j, 1) else None
                    for c in two:
                        cols = slice(c * 512, (c + 1) * 512)
                        for k in range(KB):
                            mm = three_passes(pe, up[e][:, c, :], w_hi[:, e, k], w_lo[:, e, k],
                                              hT_hi[:, k, cols], hT_lo[:, k, cols], k == 0, k == KB - 1)
                    mm.then_inc(up_ok, 1)

            def project_down(j, b, i):
                pe.wait_ge(fflo_ok, j + 1)
                for t in range(MT):
                    pe.wait_ge(add_ok, free(j * MT + t))
                    toks = slice(t * P, (t + 1) * P)
                    for c in two:
                        cols = slice(c * 512, (c + 1) * 512)
                        mm = three_passes(pe, dn[t % 2][:, c, :], ff_hi[:, b, toks], ff_lo[:, b, toks],
                                          d_hi[:, b, cols], d_lo[:, b, cols], True, True)
                    mm.then_inc(dn_ok, 1)

            over_pairs(pe, FB, project_up, project_down)

def build(nc, g):
    with ExitStack() as ctx:
        hT_hi = ctx.enter_context(nc.sbuf_tensor("hT_hi", [P, KB, T], F32R))
        hT_lo = ctx.enter_context(nc.sbuf_tensor("hT_lo", [P, KB, T], F32R))
        normalise_transpose(nc, g, "pre", g["x"], g["g_mix_pre"], hT_hi, hT_lo, NT)
        project(nc, g, hT_hi, hT_lo)
        project_values(nc, g, hT_hi, hT_lo)
        hgrn_mixer(nc, g, hT_hi, hT_lo)
    fox_prepare(nc, g)
    fox_attention(nc, g)
    retention_and_output(nc, g)
    with ExitStack() as ctx:
        hT_hi = ctx.enter_context(nc.sbuf_tensor("h2_hi", [P, KB, TH], F32R))
        hT_lo = ctx.enter_context(nc.sbuf_tensor("h2_lo", [P, KB, TH], F32R))
        halo = ctx.enter_context(nc.sbuf_tensor("halo", [P, FB, 2, 2], F32))
        for half in range(2):
            normalise_transpose(nc, g, f"ffn{half}", g["x_mid"][half * TH:(half + 1) * TH, :], g["g_ffn_pre"],
                                hT_hi, hT_lo, MT)
            mlp(nc, g, half, hT_hi, hT_lo, halo)


def shape_constants():
    f = np.float32
    t = np.arange(P)
    c = {"c_ident": np.eye(P, dtype=f)}
    c["c_negmask"] = np.where(t[:, None] >= t[None, :], f(0), f(NEG)).astype(f)
    c["c_negmaskT"] = np.ascontiguousarray(c["c_negmask"].T)
    c["c_tri"] = (t[:, None] <= t[None, :]).astype(f)
    c["c_headsum"] = np.kron(np.eye(2), np.ones((HD, HD))).astype(f)
    inv_freq = (f(1.0) / (f(10000.0) ** (np.arange(0, HD, 2, dtype=f) / f(HD)))).astype(f)
    ang = (np.arange(T, dtype=f)[:, None] * inv_freq[None, :]).astype(f)
    c["c_cos"] = np.ascontiguousarray(np.tile(np.cos(ang).T, (4, 1)).astype(f))
    c["c_sin"] = np.ascontiguousarray(np.tile(np.sin(ang).T, (4, 1)).astype(f))
    log_gamma = np.log1p(-np.exp2(-5.0 - np.arange(4)))
    rel = t[None, :] - t[:, None]
    c["c_intra"] = np.stack([np.where(rel >= 0, np.exp(lg * np.maximum(rel, 0)), 0.0)
                             for lg in log_gamma], 1).astype(f) * f(HD ** -0.5)
    rows = np.repeat(log_gamma, 32)[:, None]
    c["c_qscale"] = np.exp(rows * (t + 1.0)[None, :]).astype(f)
    c["c_kscale"] = np.exp(rows * (P - 1.0 - t)[None, :]).astype(f) * f(HD ** -0.5)
    c["c_own"] = np.kron(np.eye(4), np.ones((32, HD))).astype(f)
    c["c_cdecay"] = np.exp(rows * P).astype(f)
    c["c_hmask"] = np.kron(np.eye(4), np.ones((32, 1))).astype(f)
    lv = []
    for h in LEVELS:
        nb = P // (2 * h)
        m = np.zeros((P, nb, h), np.int32)
        for b in range(nb):
            m[2 * h * b:2 * h * b + h, b, :] = 1
        lv.append(m.reshape(P, HD))
    c["c_level"] = np.stack(lv, 1)
    c["c_diag"] = np.eye(P, dtype=np.int32)
    return c


def kernel(**inputs):
    import numpy as _np
    import concourse.bacc as _bacc
    from concourse import mybir as _mybir
    from concourse.bass_utils import run_bass_kernel_spmd as _run

    nc = _bacc.Bacc("TRN2", target_bir_lowering=False, num_devices=1)
    a = {k: _np.ascontiguousarray(v) for k, v in inputs.items()}
    w = a.pop("w_in")[0].reshape(KB, P, -1)
    lay = shape_constants()

    def block(cols):
        return w[:, :, cols].transpose(1, 0, 2)

    def run_of(start, n):
        return [_np.arange(start + P * j, start + P * (j + 1)) for j in range(n)]

    def halves(start):
        c = _np.arange(start, start + 256).reshape(4, 2, 32)
        return [c[:, 0].reshape(-1), c[:, 1].reshape(-1)]

    groups = (run_of(0, 3) + run_of(384, 3) + run_of(1152, 3) + run_of(1536, 3) + run_of(1920, 3)
              + halves(3078) + halves(3334) + run_of(3846, 2) + run_of(2694, 3))
    forget = _np.zeros((P, KB, P), w.dtype)
    forget[:, :, 0:6] = block(_np.arange(2688, 2694))
    lay["w_blk"] = _np.stack([block(c) for c in groups] + [forget])
    v_cols = _np.concatenate([_np.arange(2304, 2688), _np.arange(768, 1152), _np.arange(3590, 3846)])
    lay["w_v"] = _np.stack([block(v_cols[:512]), block(v_cols[512:])])
    up = a.pop("w_up")[0].reshape(KB, P, 2, FB, P)
    lay["w_up"] = up.transpose(3, 2, 1, 0, 4)
    lay["w_out"] = a.pop("w_out")[0].reshape(KB, P, D)
    lay["w_down"] = a.pop("w_down")[0].reshape(FB, P, D)
    lay["x"] = a.pop("x")[0]
    cw = _np.concatenate([a.pop("conv_w")[0], a.pop("conv_b")], 0)
    lay["conv"] = cw.reshape(4, 2, FB, P).transpose(3, 2, 1, 0)
    lay["fox_gain"] = _np.stack([_np.tile(a.pop("fox_q_gain")[0], 2), _np.tile(a.pop("fox_k_gain")[0], 2)], 1)
    lay["hgrn_gain"] = a.pop("hgrn_out_gain")[0].reshape(3, P).T
    lay["ret_gain"] = a.pop("ret_out_gain")[0].reshape(2, P).T
    lay["hgrn_lb"] = a.pop("hgrn_lb")[0].reshape(3, P).T
    lay["b_f"] = a.pop("b_fox_f")[0][:, None]
    lay.update(a)
    arrays = {f"in_{k}": _np.ascontiguousarray(v) for k, v in lay.items()}
    g = {k: nc.dram_tensor(f"in_{k}", arrays[f"in_{k}"].shape, _mybir.dt.from_np(arrays[f"in_{k}"].dtype),
                           kind="ExternalInput").ap() for k in lay}
    for name, shape in (("projT", (NPB, P, T)), ("v_tok", (T, 1024)), ("negF", (6, 2, T)),
                        ("qk_hi", (6, P, T)), ("qk_lo", (6, P, T)), ("M_rows", (6, 2, T)), ("mixT", (KB, P, T)),
                        ("x_mid", (T, D))):
        g[name] = nc.dram_tensor(name, shape, F32, kind="Internal").ap()
    g["out"] = nc.dram_tensor("out_0", (T, D), F32, kind="ExternalOutput").ap()
    build(nc, g)
    r = _run(nc, [arrays], core_ids=[0])
    return r.results[0]["out_0"].reshape(1, T, D)
```
